# Optimizing a Trainium2 kernel written in Bass

```python
import math
import jax, jax.numpy as jnp
from jax import lax
import numpy as np

D_MODEL = 2048
BATCH = 1
SEQ = 256
DEPTH = 1
DEC_BATCH = 1
DEC_SEQ = 32
PAST_LEN = 128

CHUNK = 64
N_META = 16
D_RNN = 2560
N_RNN_BLOCKS = 16
RNN_BLOCK = D_RNN // N_RNN_BLOCKS
CONV_W = 4
LRU_C = 8.0
N_HEADS_M = 8
DV_M = D_MODEL // N_HEADS_M
DQK_M = DV_M // 2
HQK = N_HEADS_M * DQK_M
HV = N_HEADS_M * DV_M
N_GROUPS = 4
EXPERTS_PER_GROUP = 4
N_EXPERTS = N_GROUPS * EXPERTS_PER_GROUP
TOP_K_IN_GROUP = 2
D_EXPERT = 512
IN_SIZES = (D_RNN, D_RNN, HQK, HQK, HV, HV, 2 * N_HEADS_M, D_MODEL, D_MODEL)
N_IN = 2 * D_RNN + 2 * HQK + 2 * HV + 2 * N_HEADS_M + 2 * D_MODEL
EPS = 1e-6

kernel_name = "hawk_mlstm_hmoe_streaming_step"

F32 = jnp.float32

def rmsnorm(x, w):
    xf = x.astype(F32)
    xf = xf * lax.rsqrt(jnp.mean(xf * xf, axis=-1, keepdims=True) + EPS)
    return (xf * w.astype(F32)).astype(x.dtype)

def rglru_branch(xr, gr, conv_buf, h0, conv_w, conv_b, a_w, a_b, x_w, x_b, lam):
    B, L, _ = xr.shape
    xp = jnp.concatenate([conv_buf.astype(xr.dtype), xr], axis=1)
    xc = conv_b.astype(xr.dtype) + conv_w[0] * xp[:, 0:L]
    for j in range(1, CONV_W):
        xc = xc + conv_w[j] * xp[:, j:j + L]
    new_buf = xp[:, L:]
    xb = xc.reshape(B, L, N_RNN_BLOCKS, RNN_BLOCK)
    r = jax.nn.sigmoid((jnp.einsum('blnc,ncd->blnd', xb, a_w).reshape(B, L, D_RNN) + a_b).astype(F32))
    i = jax.nn.sigmoid((jnp.einsum('blnc,ncd->blnd', xb, x_w).reshape(B, L, D_RNN) + x_b).astype(F32))
    log_a = -LRU_C * r * jax.nn.softplus(-lam.astype(F32))
    a = jnp.exp(log_a)
    u = jnp.sqrt(-jnp.expm1(2.0 * log_a)) * (i * xc.astype(F32))
    u = u.at[:, 0].add(a[:, 0] * h0.astype(F32))

    def combine(left, right):
        a1, b1 = left
        a2, b2 = right
        return a1 * a2, a2 * b1 + b2

    _, h = lax.associative_scan(combine, (a, u), axis=1)
    y = jax.nn.gelu(gr.astype(F32)) * h
    return y.astype(xr.dtype), new_buf, h[:, -1]

def mlstm_block(q, k, v, li, lf, C0, n0, m0):
    L = q.shape[1]
    b = jnp.cumsum(lf.astype(F32), axis=1).transpose(0, 2, 1)
    ig = li.astype(F32).transpose(0, 2, 1)
    m0 = m0.astype(F32)
    C0 = C0.astype(F32)
    n0 = n0.astype(F32)
    qf, kf, vf = q.astype(F32), k.astype(F32), v.astype(F32)
    causal = jnp.tril(jnp.ones((L, L), dtype=bool))
    log_w = jnp.where(causal, b[..., :, None] - b[..., None, :] + ig[..., None, :], -jnp.inf)
    log_inter = b + m0[..., None]
    m = jnp.maximum(log_inter, jnp.max(log_w, axis=-1))
    w_intra = jnp.exp(log_w - m[..., None])
    w_inter = jnp.exp(log_inter - m)
    s = jnp.einsum('bthk,bshk->bhts', qf, kf) * w_intra
    num = jnp.einsum('bhts,bshv->bthv', s, vf) + jnp.einsum('bht,bthk,bhkv->bthv', w_inter, qf, C0)
    den = jnp.sum(s, axis=-1) + w_inter * jnp.einsum('bthk,bhk->bht', qf, n0)
    denom = jnp.maximum(jnp.abs(den), jnp.exp(-m))
    h = num / denom.transpose(0, 2, 1)[..., None]
    m_end = m[..., -1]
    w_end = jnp.exp(b[..., -1:] - b + ig - m_end[..., None])
    decay = jnp.exp(b[..., -1] + m0 - m_end)
    C_new = decay[..., None, None] * C0 + jnp.einsum('bhs,bshk,bshv->bhkv', w_end, kf, vf)
    n_new = decay[..., None] * n0 + jnp.einsum('bhs,bshk->bhk', w_end, kf)
    return h, (C_new, n_new, m_end)

def mlstm_sequence(q, k, v, li, lf, C0, n0, m0, n_lead):
    h_lead, st = mlstm_block(q[:, :n_lead], k[:, :n_lead], v[:, :n_lead],
                             li[:, :n_lead], lf[:, :n_lead], C0, n0, m0)
    rest = q.shape[1] - n_lead
    if rest == 0:
        return h_lead, st
    n_blk = rest // CHUNK

    def to_blocks(a):
        a = a[:, n_lead:]
        a = a.reshape(a.shape[0], n_blk, CHUNK, *a.shape[2:])
        return jnp.moveaxis(a, 1, 0)

    def step(carry, blk):
        h, carry = mlstm_block(*blk, *carry)
        return carry, h

    blocks = (to_blocks(q), to_blocks(k), to_blocks(v), to_blocks(li), to_blocks(lf))
    st, hs = lax.scan(step, st, blocks)
    hs = jnp.moveaxis(hs, 0, 1).reshape(q.shape[0], rest, *hs.shape[3:])
    return jnp.concatenate([h_lead, hs], axis=1), st

def hier_moe(x, w_rg, b_rg, w_re, b_re, w_g, w_u, w_d):
    B, L, D = x.shape
    xf = x.reshape(B * L, D)
    g_logits = (xf @ w_rg + b_rg).astype(F32)
    g_prob = jax.nn.softmax(g_logits, axis=-1)
    g_idx = jnp.argmax(g_logits, axis=-1)
    g_w = jnp.max(g_prob, axis=-1, keepdims=True)
    e_logits = (xf @ w_re + b_re).astype(F32).reshape(-1, N_GROUPS, EXPERTS_PER_GROUP)
    e_in = jnp.einsum('tge,tg->te', e_logits, jax.nn.one_hot(g_idx, N_GROUPS, dtype=F32))
    top_v, top_i = lax.top_k(e_in, TOP_K_IN_GROUP)
    top_w = jax.nn.softmax(top_v, axis=-1) * g_w
    eid = g_idx[:, None] * EXPERTS_PER_GROUP + top_i
    gates = jnp.sum(jax.nn.one_hot(eid, N_EXPERTS, dtype=F32) * top_w[..., None], axis=1)
    out = jnp.zeros((B * L, D), F32)
    for e in range(N_EXPERTS):
        hdn = jax.nn.silu(xf @ w_g[e]) * (xf @ w_u[e])
        out = out + gates[:, e:e + 1] * (hdn @ w_d[e]).astype(F32)
    return out.astype(x.dtype).reshape(B, L, D)

def trunk_layer(x, conv_buf, h0, C0, n0, m0, n_lead, p):
    B, L, _ = x.shape
    xn = rmsnorm(x, p['norm1_w'])
    proj = xn @ p['w_in']
    cuts = []
    acc = 0
    for s in IN_SIZES[:-1]:
        acc += s
        cuts.append(acc)
    xr, gr, q, k, v, og, gif, mg_r, mg_m = jnp.split(proj, cuts, axis=-1)
    y_r, conv_new, h_new = rglru_branch(xr, gr, conv_buf, h0, p['conv_w'], p['conv_b'],
                                        p['rg_a_w'], p['rg_a_b'], p['rg_x_w'], p['rg_x_b'], p['rg_lambda'])
    q = q.reshape(B, L, N_HEADS_M, DQK_M)
    k = k.reshape(B, L, N_HEADS_M, DQK_M) * (DQK_M ** -0.5)
    v = v.reshape(B, L, N_HEADS_M, DV_M)
    gif = gif.astype(F32) + p['b_gates'].astype(F32)
    li = gif[..., :N_HEADS_M]
    lf = jax.nn.log_sigmoid(gif[..., N_HEADS_M:])
    hm, (C_new, n_new, m_new) = mlstm_sequence(q, k, v, li, lf, C0, n0, m0, n_lead)
    hm = hm * lax.rsqrt(jnp.mean(hm * hm, axis=-1, keepdims=True) + EPS)
    hm = hm * p['mlstm_norm_w'].astype(F32).reshape(N_HEADS_M, DV_M)
    y_m = (hm.reshape(B, L, HV) * jax.nn.sigmoid(og.astype(F32))).astype(x.dtype)
    mix = jax.nn.sigmoid(mg_r) * (y_r @ p['w_proj_rnn']) + jax.nn.sigmoid(mg_m) * (y_m @ p['w_proj_mlstm'])
    x = x + mix @ p['w_out']
    x = x + hier_moe(rmsnorm(x, p['norm2_w']), p['w_router_group'], p['b_router_group'],
                     p['w_router_expert'], p['b_router_expert'],
                     p['w_exp_gate'], p['w_exp_up'], p['w_exp_down'])
    dt = x.dtype
    return x, (conv_new.astype(dt), h_new.astype(dt), C_new.astype(dt), n_new.astype(dt), m_new.astype(dt))

def setup_inputs(seed: int = 0) -> dict:
    key = jax.random.key(seed)
    ks = jax.random.split(key, 40)

    def nrm(k, shape, s):
        return s * jax.random.normal(k, shape, F32)

    u = jax.random.uniform(ks[20], (DEPTH, D_RNN), F32, 0.9, 0.999)
    a0 = u ** (1.0 / LRU_C)
    rg_lambda = jnp.log(a0) - jnp.log1p(-a0)
    b_i = nrm(ks[21], (DEPTH, N_HEADS_M), 0.1)
    b_f = jnp.linspace(3.0, 6.0, N_HEADS_M, dtype=F32)[None] + nrm(ks[22], (DEPTH, N_HEADS_M), 0.1)
    return {
        "x_prompt": nrm(ks[0], (BATCH, SEQ, D_MODEL), 1.0),
        "x_sample": nrm(ks[1], (DEC_BATCH, DEC_SEQ, D_MODEL), 1.0),
        "state_rglru_conv": nrm(ks[2], (DEPTH, DEC_BATCH, CONV_W - 1, D_RNN), 1.0),
        "state_rglru_h": nrm(ks[3], (DEPTH, DEC_BATCH, D_RNN), 0.5),
        "state_mlstm_C": nrm(ks[4], (DEPTH, DEC_BATCH, N_HEADS_M, DQK_M, DV_M), 0.05),
        "state_mlstm_n": nrm(ks[5], (DEPTH, DEC_BATCH, N_HEADS_M, DQK_M), 0.05),
        "state_mlstm_m": nrm(ks[6], (DEPTH, DEC_BATCH, N_HEADS_M), 0.5),
        "meta_tokens": nrm(ks[7], (N_META, D_MODEL), 1.0),
        "norm1_w": 1.0 + nrm(ks[8], (DEPTH, D_MODEL), 0.02),
        "w_in": nrm(ks[9], (DEPTH, D_MODEL, N_IN), D_MODEL ** -0.5),
        "b_gates": jnp.concatenate([b_i, b_f], axis=-1),
        "conv_w": nrm(ks[10], (DEPTH, CONV_W, D_RNN), 0.5),
        "conv_b": nrm(ks[11], (DEPTH, D_RNN), 0.01),
        "rg_a_w": nrm(ks[12], (DEPTH, N_RNN_BLOCKS, RNN_BLOCK, RNN_BLOCK), RNN_BLOCK ** -0.5),
        "rg_a_b": nrm(ks[13], (DEPTH, D_RNN), 0.01),
        "rg_x_w": nrm(ks[14], (DEPTH, N_RNN_BLOCKS, RNN_BLOCK, RNN_BLOCK), RNN_BLOCK ** -0.5),
        "rg_x_b": nrm(ks[15], (DEPTH, D_RNN), 0.01),
        "rg_lambda": rg_lambda,
        "mlstm_norm_w": 1.0 + nrm(ks[16], (DEPTH, HV), 0.02),
        "w_proj_rnn": nrm(ks[17], (DEPTH, D_RNN, D_MODEL), D_RNN ** -0.5),
        "w_proj_mlstm": nrm(ks[18], (DEPTH, HV, D_MODEL), HV ** -0.5),
        "w_out": nrm(ks[19], (DEPTH, D_MODEL, D_MODEL), D_MODEL ** -0.5),
        "norm2_w": 1.0 + nrm(ks[23], (DEPTH, D_MODEL), 0.02),
        "w_router_group": nrm(ks[24], (DEPTH, D_MODEL, N_GROUPS), D_MODEL ** -0.5),
        "b_router_group": nrm(ks[25], (DEPTH, N_GROUPS), 0.01),
        "w_router_expert": nrm(ks[26], (DEPTH, D_MODEL, N_EXPERTS), D_MODEL ** -0.5),
        "b_router_expert": nrm(ks[27], (DEPTH, N_EXPERTS), 0.01),
        "w_exp_gate": nrm(ks[28], (DEPTH, N_EXPERTS, D_MODEL, D_EXPERT), D_MODEL ** -0.5),
        "w_exp_up": nrm(ks[29], (DEPTH, N_EXPERTS, D_MODEL, D_EXPERT), D_MODEL ** -0.5),
        "w_exp_down": nrm(ks[30], (DEPTH, N_EXPERTS, D_EXPERT, D_MODEL), D_EXPERT ** -0.5),
        "norm_f_w": 1.0 + nrm(ks[31], (D_MODEL,), 0.02),
    }

def reference(x_prompt, x_sample, state_rglru_conv, state_rglru_h, state_mlstm_C, state_mlstm_n,
              state_mlstm_m, meta_tokens, norm1_w, w_in, b_gates, conv_w, conv_b, rg_a_w, rg_a_b,
              rg_x_w, rg_x_b, rg_lambda, mlstm_norm_w, w_proj_rnn, w_proj_mlstm, w_out, norm2_w,
              w_router_group, b_router_group, w_router_expert, b_router_expert, w_exp_gate,
              w_exp_up, w_exp_down, norm_f_w):
    B = x_prompt.shape[0]
    dt = x_prompt.dtype
    xp = jnp.concatenate([jnp.broadcast_to(meta_tokens.astype(dt)[None], (B, N_META, D_MODEL)), x_prompt], axis=1)
    xs = x_sample
    n_lead_sample = x_sample.shape[1]
    p_conv, p_h, p_C, p_n, p_m = [], [], [], [], []
    s_conv, s_h, s_C, s_n, s_m = [], [], [], [], []
    for l in range(DEPTH):
        p = dict(norm1_w=norm1_w[l], w_in=w_in[l], b_gates=b_gates[l], conv_w=conv_w[l], conv_b=conv_b[l],
                 rg_a_w=rg_a_w[l], rg_a_b=rg_a_b[l], rg_x_w=rg_x_w[l], rg_x_b=rg_x_b[l],
                 rg_lambda=rg_lambda[l], mlstm_norm_w=mlstm_norm_w[l], w_proj_rnn=w_proj_rnn[l],
                 w_proj_mlstm=w_proj_mlstm[l], w_out=w_out[l], norm2_w=norm2_w[l],
                 w_router_group=w_router_group[l], b_router_group=b_router_group[l],
                 w_router_expert=w_router_expert[l], b_router_expert=b_router_expert[l],
                 w_exp_gate=w_exp_gate[l], w_exp_up=w_exp_up[l], w_exp_down=w_exp_down[l])
        xp, st_p = trunk_layer(xp,
                               jnp.zeros((B, CONV_W - 1, D_RNN), dt),
                               jnp.zeros((B, D_RNN), F32),
                               jnp.zeros((B, N_HEADS_M, DQK_M, DV_M), F32),
                               jnp.zeros((B, N_HEADS_M, DQK_M), F32),
                               jnp.zeros((B, N_HEADS_M), F32),
                               N_META, p)
        xs, st_s = trunk_layer(xs, state_rglru_conv[l], state_rglru_h[l], state_mlstm_C[l],
                               state_mlstm_n[l], state_mlstm_m[l], n_lead_sample, p)
        p_conv.append(st_p[0]); p_h.append(st_p[1]); p_C.append(st_p[2]); p_n.append(st_p[3]); p_m.append(st_p[4])
        s_conv.append(st_s[0]); s_h.append(st_s[1]); s_C.append(st_s[2]); s_n.append(st_s[3]); s_m.append(st_s[4])
    y_prompt = rmsnorm(xp, norm_f_w)[:, N_META:]
    y_sample = rmsnorm(xs, norm_f_w)
    return (y_prompt, y_sample,
            jnp.stack(p_conv), jnp.stack(p_h), jnp.stack(p_C), jnp.stack(p_n), jnp.stack(p_m),
            jnp.stack(s_conv), jnp.stack(s_h), jnp.stack(s_C), jnp.stack(s_n), jnp.stack(s_m))


_drawn_inputs = setup_inputs


def setup_inputs(seed=0):
    import zlib

    import numpy as np

    out = dict(_drawn_inputs(seed))
    spreads = {}
    factors = {'rg_a_b': 23.537,
     'rg_x_b': 8.0,
     'mlstm_norm_w': 4.169,
     'b_router_group': 4.352,
     'b_router_expert': 17.966,
     'norm_f_w': 8.28,
     'norm2_w': 3.421}
    for name, (base, spread) in spreads.items():
        noise = np.random.default_rng([zlib.crc32(name.encode()), seed]).standard_normal(out[name].shape)
        drawn = base * np.exp(spread * noise) if base else spread * noise
        out[name] = __import__('jax').numpy.asarray(drawn.astype(out[name].dtype))
    for name, factor in factors.items():
        out[name] = (out[name] * factor).astype(out[name].dtype)
    return out
```

```python
def build(nc, A, O):
    import concourse.bass as bass
    from concourse import mybir
    from contextlib import ExitStack

    F32, I32, U32, F32R = mybir.dt.float32, mybir.dt.int32, mybir.dt.uint32, mybir.dt.float32r
    ACT, ALU, AX = mybir.ActivationFunctionType, mybir.AluOpType, mybir.AxisListType
    P = 128

    NM, DM = A["meta_tokens"].shape
    NP, NS = A["x_prompt"].shape[1], A["x_sample"].shape[1]
    TP = NM + NP
    T = TP + NS
    DR = A["conv_w"].shape[2]
    CW = A["conv_w"].shape[1]
    NB, RB = A["rg_a_w"].shape[1], A["rg_a_w"].shape[2]
    NH, DQK, DV = A["state_mlstm_C"].shape[2:]
    NG, NE = A["w_router_group"].shape[2], A["w_router_expert"].shape[2]
    EG = NE // NG
    DE = A["w_exp_gate"].shape[3]
    EPS = 1e-6
    KD = DM // P
    KR = DR // P
    KE = DE // P
    TT = [(0, P), (P, P), (2 * P, T - 2 * P)]
    NL = TT[2][1]
    PL = TP - 2 * P
    G = 4
    GT = KR // G
    BG = NB // G
    PADDED = T + 2 * (CW - 1)
    CONV = PADDED - (CW - 1)
    S0 = TP + CW - 1
    SEED = 4
    NEG = -1e30
    C_Q = 2 * DR
    C_V = C_Q + 2 * NH * DQK
    C_OG = C_V + NH * DV
    C_GIF = C_OG + NH * DV
    C_MG = C_GIF + 2 * NH
    CAP = P // 2
    NPAIR = NE // 2
    MAXR = -(-T // CAP)
    ROUND_ROWS = NE * CAP
    SLOTS = MAXR * ROUND_ROWS

    w_in = A["w_in"][0].rearrange("(k p) n -> p k n", p=P)
    w_pr = A["w_proj_rnn"][0].rearrange("(k p) n -> p k n", p=P)
    w_pm = A["w_proj_mlstm"][0].rearrange("(k p) n -> p k n", p=P)
    w_out = A["w_out"][0].rearrange("(k p) n -> p k n", p=P)
    w_eg = A["w_exp_gate"][0].rearrange("e (k p) n -> p e k n", p=P)
    w_eu = A["w_exp_up"][0].rearrange("e (k p) n -> p e k n", p=P)
    w_ed = A["w_exp_down"][0].rearrange("e (k p) n -> p e k n", p=P)

    xn2_rows = nc.dram_tensor("xn2_rows", (T, DM), F32)
    slot_token = nc.dram_tensor("slot_token", (SLOTS + P, 1), I32)
    slot_out = nc.dram_tensor("slot_out", (SLOTS, DM), F32)

    ctx = ExitStack()
    with ctx:
        place = {}

        def sb(name, shape, dt=F32):
            place[name] = (nc.sbuf_base + 31) // 32 * 32
            return ctx.enter_context(nc.sbuf_tensor(name, shape, dt))

        def rounded(name, host, at, words):
            return nc.alloc_sbuf_tensor_at(name, [P, words], F32R, offset=place[host] + 4 * at)[:, :]

        def sem(name):
            return ctx.enter_context(nc.semaphore(name))

        def bcast(row):
            return row.partition_broadcast(P)

        UW = KD * 2 * P
        ring = sb("ring", [P, 4, UW])
        XNT = sb("XNT", [P, KD, T])
        OG = sb("OG", [P, KD, T])
        BW = 2 * T + 3 * DV
        HB = sb("HB", [P, NH, BW])
        XG = sb("XG", [P, 2 * KR, PADDED])
        ident = sb("ident", [P, P])
        ones = sb("ones", [P, P])
        before = sb("before", [P, P])
        tri = sb("tri", [P, TP])
        trl = sb("trl", [NL, NL])
        vec = sb("vec", [P, 320])
        CL = sb("CL", [P, KR])
        wgif = sb("wgif", [P, KD, 2 * NH])
        wrt = sb("wrt", [P, KD, NG + NE])
        AB = sb("AB", [P, GT, CONV])
        ST = sb("ST", [P, 2, CW * KR])
        small = sb("small", [P, 24])
        gtok = sb("gtok", [P, 3, 3 * NH])
        hb16 = sb("hb16", [P, 2 * NH])
        nst = sb("nst", [P, 3 * NH])
        gates8 = sb("gates8", [NH, 12])

        XGf = XG[:, :, :].rearrange("p a b -> p (a b)")
        HBf = HB[:, :, :].rearrange("p a b -> p (a b)")
        OGf = OG[:, :, :].rearrange("p a b -> p (a b)")
        HALF = 3 * DM
        xtok = XGf[:, 0:HALF].rearrange("p (a b) -> p a b", a=3)
        xntok = XGf[:, HALF:2 * HALF].rearrange("p (a b) -> p a b", a=3)
        vstage = HBf[:, 0:3 * P].rearrange("p (a b) -> p a b", a=3)
        junk = HBf[:, 512:512 + DM]

        HV0 = 2 * T
        bd = [[HB[:, i, HV0 + m * 3 * P:HV0 + (m + 1) * 3 * P] for i in range(GT)] for m in range(2)]
        RT = [HB[:, GT + j // 2, HV0 + (j % 2) * 3 * P:HV0 + (j % 2) * 3 * P + CONV] for j in range(GT)]
        tmp = HB[:, NH - 1, HV0 + 3 * P:HV0 + 3 * P + CONV]

        at = [0]

        def ml(n):
            at[0] += n
            assert at[0] <= KR * PADDED
            return XGf[:, at[0] - n:at[0]]
        negM, expnm = ml(T), ml(T)
        rows0 = at[0]
        kh, qh, vh = ml(T), ml(T), ml(3 * DV)
        DW = T + TP - P - NS + NL
        dw, hh, sq = ml(DW), ml(2 * T), ml(2 * T)
        rd, es, kp, ks = ml(T), ml(T), ml(3 * DQK), ml(DQK)
        c0, cn = ml(DV), ml(2 * DV)
        selM, selE = ml(T), ml(T)
        at[0] = rows0
        li, lf, bc, gg, wp, ws, t0, t1 = (ml(T)[0:NH] for _ in range(8))
        small2 = sb("small2", [P, NS])
        kc = sb("kc", [P, NE + EG])
        tokid = sb("tokid", [P, 3], I32)
        nrounds = sb("nrounds", [P, 1], I32)
        slot_i = sb("slot_i", [P, 2, 3], I32)
        gidx = sb("gidx", [P, 1], I32)
        RTW = sb("RTW", [P, 6])

        bank = [ctx.enter_context(nc.psum_tensor(f"bank{i}", [P, 512], F32)) for i in range(8)]

        V_N1, V_N2, V_MN, V_CB = 0, KD, 2 * KD, 3 * KD
        V_AB, V_XB, V_LM = V_CB + KR, V_CB + 2 * KR, V_CB + 3 * KR
        V_CW, V_H0, V_CS = P, P + CW * KR, 2 * P

        SC = [(P, 0, TP, 0), (P, TP, TP - P, P), (NL, TP + TP - P, NL, 2 * P)]

        slot_full = [sem(f"slot_full{b}") for b in range(4)]
        groups_done, dve_evac, act_evac = sem("groups_done"), sem("dve_evac"), sem("act_evac")
        dve_steps, act_steps = sem("dve_steps"), sem("act_steps")

        n0b = sq[:, 0:P]
        diag8 = sb("diag8", [NH, 2 * NH])[:, :]
        zeros_i = sb("zeros_i", [P, (SLOTS + P) // P], I32)
        junk2 = HBf[:, 8000:8000 + DM]
        xn2t = HBf[:, KD // 4 * BW:KD // 4 * BW + KD * T].rearrange("p (k t) -> p k t", k=KD)
        rows = HBf[:, 0:DM]
        xs = rounded("xs", "HB", DM, 2 * DM).rearrange("p (k e c) -> p k e c", k=KD, e=2)
        ysb = HBf[:, 3 * DM:5 * DM].rearrange("p (e n) -> p e n", e=2)
        w_raw = [ring[:, b, :] for b in range(4)]
        w_low = [rounded(f"w_low{b}", "ring", b * UW, UW) for b in range(4)]
        XKf = XGf[:, HALF:2 * HALF]
        w_high = [rounded("w_high0", "XNT", 0, UW), rounded("w_high1", "XG", HALF, UW)]
        HC = KE * CAP
        gu = XKf[:, UW:UW + 2 * DE].rearrange("p (a n) -> p a n", a=2)
        sg = XKf[:, UW + 2 * DE:UW + 2 * DE + HC]
        hf = XKf[:, UW + 2 * DE + HC:UW + 2 * DE + 2 * HC]
        hs_high = rounded("hs_high", "XG", HALF + UW + 2 * DE + 2 * HC, HC)
        hs_low = rounded("hs_low", "XG", HALF + UW + 2 * DE + 3 * HC, HC)
        add2 = tri[:, 0:CAP]
        y1 = xntok
        y2 = HBf[:, 0:HALF].rearrange("p (a b) -> p a b", a=3)
        nb2, nbf = OGf[:, 0:DM], OGf[:, DM:2 * DM]
        rt_at = [2 * DM]

        def rt(n, a=3):
            rt_at[0] += a * n
            assert rt_at[0] <= KD * T
            return OGf[:, rt_at[0] - a * n:rt_at[0]].rearrange("p (a n) -> p a n", a=a)
        brt = rt(NG + NE, 1)[:, 0, :]
        gl, el = rt(NG), rt(NE)
        gmx, gkey, goh = rt(1), rt(NG), rt(NG)
        prod = rt(NE)
        ein, ekey, o1, o2, e2 = rt(EG), rt(EG), rt(EG), rt(EG), rt(EG)
        v1, v2, gw, ex, kmx = rt(1), rt(1), rt(1), rt(1), rt(1)
        E1, E2, picked = rt(NE), rt(NE), rt(NE)
        rk, sl, slt = rt(NE), rt(NE), rt(NE)
        w1, w2, slf = rt(1), rt(1), rt(2)
        cmx = rt(2, 1)[:, 0, :]

        PIECES = []
        for b_ in range(BG):
            r_ = RB * b_
            while r_ < RB * (b_ + 1):
                n_ = min(RB * (b_ + 1), (r_ // P + 1) * P) - r_
                PIECES.append((b_, r_ - RB * b_, n_, r_ // P, r_ % P))
                r_ += n_
        TOUCH = {(i, j) for (b_, _, _, i, _) in PIECES for j in range(GT)
                 if j * P < RB * (b_ + 1) and (j + 1) * P > RB * b_}
        BDP = len(PIECES)
        GATE_SEED = GT + 1
        VA_ROWS, VB_ROWS, VC_ROWS = 3 * KD + 4 * KR, CW * KR + KR, (CW - 1) * KR
        NVEC, NPAR = 10, 6
        G_QK = 2 * KR
        G_V = G_QK + 8 * G
        G_MG = G_V + 3 * NH
        G_PR = G_MG + 2 * KD
        G_PM = G_PR + KD
        G_OUT = G_PM + KD
        G_MOE = G_OUT + KD
        TURNS = 2 * KR // 8 + G + 2 + 4 + KD // 4 + 2 * (KD // 8)
        LOADS_MOE = [TURNS] * 4
        bd_loaded = [sem("bd_loaded_a"), sem("bd_loaded_x")]
        rounds_ready = sem("rounds_ready")
        gate_mm = sem("gate_mm")
        consts_ready = sem("consts_ready")
        vec_loaded = sem("vec_loaded")
        vec_transposed = sem("vec_transposed")
        xn_ready = sem("xn_ready")
        xnt_ready = sem("xnt_ready")
        x_transposed = sem("x_transposed")
        conv_done = sem("conv_done")
        gate_evac = sem("gate_evac")
        par_loaded = sem("par_loaded")
        gif_done = sem("gif_done")
        rows_t = sem("rows_t")
        gt_mm = sem("gt_mm")
        gt_ready = sem("gt_ready")
        staged_a = sem("staged_a")
        staged_d = sem("staged_d")
        pe_scores = sem("pe_scores")
        sw_ready = sem("sw_ready")
        es_ready = sem("es_ready")
        c0_loaded = sem("c0_loaded")
        pe_num = sem("pe_num")
        pe_kt = sem("pe_kt")
        h_ready = sem("h_ready")
        sq_h = sem("sq_h")
        pe_ss = sem("pe_ss")
        kp_ready = sem("kp_ready")
        pe_cn = sem("pe_cn")
        group_done = sem("group_done")
        head_done = sem("head_done")
        st_t = sem("st_t")
        x2_ready = sem("x2_ready")
        x2_t = sem("x2_t")
        xn2_ready = sem("xn2_ready")
        xn2t_ready = sem("xn2t_ready")
        xn2_t = sem("xn2_t")
        st_ready = sem("st_ready")
        logits = sem("logits")
        chosen = sem("chosen")
        rank_mm = sem("rank_mm")
        rows_gathered = sem("rows_gathered")
        rows_t_done = sem("rows_t_done")
        xgt_ready = sem("xgt_ready")
        h_act = sem("h_act")
        w_split = sem("w_split")
        add2_ready = sem("add2_ready")
        w_rest = sem("w_rest")
        gu_copied = sem("gu_copied")
        gu_summed = sem("gu_summed")
        xs_high = sem("xs_high")
        h_steps = sem("h_steps")
        y_out = sem("y_out")
        y_free = sem("y_free")
        x_loaded = sem("x_loaded")
        ss_init = sem("ss_init")
        ss_done = sem("ss_done")
        var_ready = sem("var_ready")
        std_ready = sem("std_ready")
        lam_abs = sem("lam_abs")
        lam_exp = sem("lam_exp")
        gelu_done = sem("gelu_done")
        gated = sem("gated")
        a_ready = sem("a_ready")
        sq_ready = sem("sq_ready")
        sqrt_done = sem("sqrt_done")
        z_abs = sem("z_abs")
        z_exp = sem("z_exp")
        mrow_ready = sem("mrow_ready")
        row_exp = sem("row_exp")
        og_ready = sem("og_ready")
        d_ready = sem("d_ready")
        wi_ready = sem("wi_ready")
        w_ready = sem("w_ready")
        vr_ready = sem("vr_ready")
        sr_ready = sem("sr_ready")
        mg_ready = sem("mg_ready")
        cn_stored = sem("cn_stored")
        nb_loaded = sem("nb_loaded")
        ss2_done = sem("ss2_done")
        var2 = sem("var2")
        std2 = sem("std2")
        cols_e = sem("cols_e")
        exps_e = sem("exps_e")
        silu_done = sem("silu_done")
        fin_ss = sem("fin_ss")
        fin_sq = sem("fin_sq")
        fin_var = sem("fin_var")
        fin_std = sem("fin_std")
        cn_ready = sem("cn_ready")
        vec_ready = sem("vec_ready")
        states_saved = sem("states_saved")
        xr_loaded = sem("xr_loaded")
        y_loaded = sem("y_loaded")
        fin_out = sem("fin_out")
        zeroed = sem("zeroed")
        out_stored = sem("out_stored")
        xn2_stored = sem("xn2_stored")
        perm_written = sem("perm_written")
        rest_zeroed = sem("rest_zeroed")
        idx_loaded = sem("idx_loaded")
        y_stored = sem("y_stored")
        pool_steps = sem("pool_steps")

        def wait_apart(eng, reached, counter, value):
            value = eng.to_reg(value)
            eng.wait_ge(reached, 1)
            eng.wait_ge(counter, value)

        class Steps:

            def __init__(self, eng, counter):
                self.eng, self.counter, self.base, self.n = eng, counter, 0, 0

            def step(self, ins, beside=None):
                ins.then_inc(self.counter, 1)
                self.n += 1
                if beside is None:
                    self.eng.wait_ge(self.counter, self.base + self.n)
                else:
                    wait_apart(self.eng, beside, self.counter, self.base + self.n)

            def enter(self, i, per):
                self.start, self.per = self.base + self.n, per
                self.base, self.n = self.start + i * per, 0

            def leave(self, count):
                assert self.n == self.per, (self.n, self.per)
                self.base, self.n = self.start + count * self.per, 0

        block = ctx.enter_context(nc.Block())

        @block.sync
        def _(sp):
            freed = [None] * 4

            def stream(iters, groups, start, unit):
                def load(i, b):
                    dst, src = unit(i, b)
                    sp.dma_start(dst, src).then_inc(slot_full[b], 16)
                for b in range(4):
                    if freed[b] is not None:
                        sp.wait_ge(groups_done, freed[b])
                    load(0, b)
                if iters > 1:
                    with sp.Fori(0, iters - 1) as i:
                        for b in range(4):
                            sp.wait_ge(groups_done, i * (4 * groups) + start + (b + 1) * groups)
                            load(i + 1, b)
                for b in range(4):
                    freed[b] = start + (iters - 1) * 4 * groups + (b + 1) * groups
                return start + iters * 4 * groups

            def full(b):
                return ring[:, b, :].rearrange("p (k n) -> p k n", k=KD)

            def wide(w, first):
                return lambda i, b: (full(b), w[:, :, bass.ds(i * (8 * P) + (first + b * 2 * P), 2 * P)])

            g = stream(2 * KR // 8, 2, 0, wide(w_in, 0))
            g = stream(2, 2, g, wide(w_in, C_Q))
            g = stream(2, 2, g, wide(w_in, C_OG))
            g = stream(2, 3, g, wide(w_in, C_V))
            g = stream(4, 2, g, wide(w_in, C_MG))
            g = stream(KD // 4, 1, g, lambda i, b: (
                ring[:, b, 0:KR * P].rearrange("p (k n) -> p k n", k=KR),
                w_pr[:, :, bass.ds(i * (4 * P) + b * P, P)]))
            g = stream(KD // 8, 2, g, wide(w_pm, 0))
            g = stream(KD // 8, 2, g, wide(w_out, 0))
            assert g == G_MOE

            def expert_unit(e, k):
                if k < 4:
                    w, h = (w_eg if k < 2 else w_eu), KD // 2
                    return w[:, e, (k % 2) * h:(k % 2 + 1) * h, :].rearrange("p e k n -> p (e k) n")
                hw = DM // 2
                return w_ed[:, e, :, (k - 4) * hw:(k - 3) * hw].rearrange("p e k n -> p (e k) n")

            def unit_view(b, k):
                return ring[:, b, :].rearrange("p (k n) -> p k n", k=(KD // 2 if k < 4 else KE))

            for b in range(4):
                sp.wait_ge(groups_done, freed[b])
                sp.dma_start(unit_view(b, b), expert_unit(slice(0, 1), b)).then_inc(slot_full[b], 16)
            sp.wait_ge(rounds_ready, 1)
            n = sp.value_load(nrounds[0:1, 0:1], min_val=1, max_val=MAXR)
            with sp.Fori(0, n) as r:
                with sp.Fori(0, NPAIR) as q:
                    for u in range(4, 12):
                        sp.wait_ge(groups_done, (r * NPAIR + q) * 12 + (G_MOE + u - 3))
                        sp.dma_start(unit_view(u % 4, u % 6), expert_unit(bass.ds(q * 2 + u // 6, 1), u % 6)
                                     ).then_inc(slot_full[u % 4], 16)
                    nq = (q + 1) % NPAIR
                    for b in range(4):
                        sp.wait_ge(groups_done, (r * NPAIR + q) * 12 + (G_MOE + 8 + b + 1))
                        sp.dma_start(unit_view(b, b), expert_unit(bass.ds(nq * 2, 1), b)).then_inc(slot_full[b], 16)
            for b in range(4):
                wait_apart(sp, rounds_ready, slot_full[b], n * (NPAIR * 3 * 16) + (LOADS_MOE[b] + 1) * 16)

        @block.tensor
        def _(pe):
            for counter in (pe_scores, pe_kt, pe_num, pe_ss, pe_cn):
                pe.sem_inc(counter, 1)
            pe.sem_inc(gate_mm, GATE_SEED)

            pe.wait_ge(consts_ready, 1)
            pe.wait_ge(vec_loaded, 16 * NVEC)
            for c, n in ((0, P), (1, VB_ROWS), (2, VC_ROWS)):
                last = pe.transpose(bank[4][:, c * P:c * P + n], vstage[0:n, c, :], ident[0:n, 0:n])
            last.then_inc(vec_transposed, 1)
            pe.wait_ge(xn_ready, 3)
            for k in range(KD):
                if k >= 4:
                    pe.wait_ge(xnt_ready, k - 3)
                for i, (t, n) in enumerate(TT):
                    last = pe.transpose(bank[k % 4][:, t:t + n], xntok[0:n, i, k * P:(k + 1) * P], ident[0:n, 0:n])
                last.then_inc(x_transposed, 1)
            pe.wait_ge(xnt_ready, KD)

            def dense(i, turn, jj, evac, seen, rhs, nk=KD, tiles=2):
                b = jj // tiles
                if jj % tiles == 0:
                    pe.wait_ge(slot_full[b], (i + (turn + 1)) * 16)
                pe.wait_ge(evac, i * (4 * tiles) + (seen + jj + SEED - 3))
                w = ring[:, b, 0:nk * tiles * P].rearrange("p (k n) -> p k n", k=nk)
                c = (jj % tiles) * P
                for k in range(nk):
                    last = pe.matmul(bank[jj % 4][:, 0:T], w[:, k, c:c + P], rhs(k), start=(k == 0), stop=(k == nk - 1))
                last.then_inc(groups_done, 1)

            def xnt(k):
                return XNT[:, k, :]

            turn = 0
            n = 2 * KR // 8
            with pe.Fori(0, n) as i:
                for jj in range(8):
                    dense(i, turn, jj, dve_evac, 0, xnt)
            turn += n
            dve_seen, act_seen = 2 * KR, 0
            pe.wait_ge(dve_evac, SEED + dve_seen)

            with pe.Fori(0, G) as g:
                for m in range(2):
                    for jj in range(4 * m, 4 * m + 4):
                        dense(g, turn, jj, act_evac, act_seen, xnt)
                    pe.wait_ge(bd_loaded[m], (g + 1) * (16 * BDP))
                    pe.wait_ge(conv_done, (g + 1) * GT)
                    for j in range(GT):
                        pe.wait_ge(gate_evac, g * (2 * GT) + (SEED + m * GT + (1 if j == 4 else 0)))
                        src = [i for i in (j - 1, j, j + 1) if (i, j) in TOUCH]
                        for i in src:
                            last = pe.matmul(bank[4 + j % 4][:, 0:CONV], bd[m][i][:, (j - i + 1) * P:(j - i + 2) * P],
                                             XG[:, bass.ds(g * GT + i, 1), 0:CONV].rearrange("p a t -> p (a t)"),
                                             start=(i == src[0]), stop=(i == src[-1]))
                        last.then_inc(gate_mm, 1)
            turn += G
            act_seen += 8 * G
            pe.wait_ge(act_evac, SEED + act_seen)

            pe.wait_ge(par_loaded, 16 * NPAR)
            pe.wait_ge(gate_evac, SEED + 2 * KR)
            for c in range(2):
                for k in range(KD):
                    last = pe.matmul(bank[4 + c][0:NH, 0:T], wgif[:, k, c * NH:(c + 1) * NH], XNT[:, k, :],
                                     start=(k == 0), stop=(k == KD - 1))
                last.then_inc(gif_done, 1)

            with pe.Fori(0, 2) as i:
                for b in range(4):
                    pe.wait_ge(slot_full[b], (i + (turn + 1)) * 16)
                    for c, (t, n) in enumerate(TT):
                        jj = b * 3 + c
                        pe.wait_ge(dve_evac, i * 12 + (dve_seen + jj + SEED - 3))
                        for k in range(KD):
                            last = pe.matmul(bank[jj % 4][0:n, 0:2 * P], XNT[:, k, t:t + n],
                                             ring[:, b, k * 2 * P:(k + 1) * 2 * P], start=(k == 0), stop=(k == KD - 1))
                        last.then_inc(groups_done, 1)
            turn += 2
            dve_seen += 24
            pe.wait_ge(dve_evac, SEED + dve_seen)

            pe.wait_ge(rows_t, 1)
            for c, row in enumerate((gg, wp, ws)):
                for i, (t, n) in enumerate(TT):
                    pe.transpose(bank[6][0:n, (i * 3 + c) * NH:(i * 3 + c + 1) * NH], row[:, t:t + n], ident[0:NH, 0:NH])
            pe.matmul(bank[7][:, 0:2 * NH], ones[0:NH, :], diag8, start=True, stop=True).then_inc(gt_mm, 1)
            pe.wait_ge(gt_ready, 1)

            with pe.Fori(0, NH // 2) as hp:
                for e in range(2):
                    h1 = hp * 2 + (e + 1)
                    dense(hp, turn, 4 * e, act_evac, act_seen, xnt)
                    pe.wait_ge(staged_a, h1)
                    pe.wait_ge(staged_d, h1)
                    for m, c, n, t in SC:
                        pe.matmul(bank[4][0:m, c:c + n], kh[:, t:t + m], qh[:, t:t + n], start=True, stop=True)
                    pe.matmul(bank[5][:, 0:T], ones[0:NH, :], selM[0:NH], start=True, stop=True)
                    pe.matmul(bank[6][:, 0:T], ones[0:NH, :], selE[0:NH], start=True, stop=True).then_inc(pe_scores, 1)
                    dense(hp, turn, 4 * e + 1, act_evac, act_seen, xnt)
                    pe.wait_ge(sw_ready, h1)
                    pe.wait_ge(es_ready, h1)
                    pe.wait_ge(c0_loaded, h1 * 16)
                    for b, lt in ((5, None), (6, 0), (7, 1)):
                        def left(i, n):
                            return ones[0:n, :] if lt is None else vh[0:n, i * DV + lt * P:i * DV + (lt + 1) * P]
                        pe.matmul(bank[b][:, 0:TP], left(0, P), dw[:, 0:TP], start=True, stop=False)
                        pe.matmul(bank[b][:, P:TP], left(1, P), dw[:, TP:TP + TP - P], start=False, stop=False)
                        c = SC[2][1]
                        pe.matmul(bank[b][:, 2 * P:TP], left(2, NL), dw[0:NL, c:c + PL], start=False, stop=False)
                        pe.matmul(bank[b][:, TP:T], left(2, NL), dw[0:NL, c + PL:c + NL], start=False, stop=False)
                        l0 = n0b if lt is None else c0[:, lt * P:(lt + 1) * P]
                        last = pe.matmul(bank[b][:, TP:T], l0, small2[:, :], start=False, stop=True)
                    last.then_inc(pe_num, 1)
                    dense(hp, turn, 4 * e + 2, act_evac, act_seen, xnt)
                    for i, (t, n) in enumerate(TT):
                        last = pe.transpose(bank[4][0:n, i * P:(i + 1) * P], kh[:, t:t + n], ident[:, :])
                    last.then_inc(pe_kt, 1)
                    pe.wait_ge(h_ready, h1)
                    pe.wait_ge(sq_h, h1)
                    for c in range(2):
                        last = pe.matmul(bank[5][:, 0:T], ones[:, :], sq[:, c * T:(c + 1) * T], start=(c == 0), stop=(c == 1))
                    last.then_inc(pe_ss, 1)
                    dense(hp, turn, 4 * e + 3, act_evac, act_seen, xnt)
                    pe.wait_ge(kp_ready, h1)
                    for c, rhs in ((0, None), (1, ones)):
                        dst = bank[6][:, 0:DV] if c == 0 else bank[7][:, 0:1]
                        for i, (t, n) in enumerate(TT):
                            r_ = vh[0:n, i * DV:(i + 1) * DV] if c == 0 else ones[0:n, 0:1]
                            pe.matmul(dst, kp[0:n, i * DQK:(i + 1) * DQK], r_, start=(i == 0), stop=(i == 2))
                        dst = bank[6][:, DV:2 * DV] if c == 0 else bank[7][:, 1:2]
                        r_ = vh[0:NL, 2 * DV:3 * DV] if c == 0 else ones[0:NL, 0:1]
                        last = pe.matmul(dst, ks[0:NL, :], r_, start=True, stop=True)
                    last.then_inc(pe_cn, 1)
            turn += 4
            act_seen += 2 * KD
            pe.wait_ge(act_evac, SEED + act_seen)

            def yr(k):
                return XG[:, KR + k, 0:T]

            def ym(k):
                return OG[:, k, :]

            def mixed(k):
                return HB[:, k // 4, (k % 4) * T:(k % 4 + 1) * T]

            pe.wait_ge(group_done, G + 1)
            with pe.Fori(0, KD // 4) as i:
                for jj in range(4):
                    dense(i, turn, jj, dve_evac, dve_seen, yr, nk=KR, tiles=1)
            turn += KD // 4
            dve_seen += KD
            pe.wait_ge(head_done, NH)
            with pe.Fori(0, KD // 8) as i:
                for jj in range(8):
                    dense(i, turn, jj, dve_evac, dve_seen, ym)
            turn += KD // 8
            dve_seen += KD
            pe.wait_ge(dve_evac, SEED + dve_seen)
            with pe.Fori(0, KD // 8) as i:
                for jj in range(8):
                    dense(i, turn, jj, dve_evac, dve_seen, mixed)
            turn += KD // 8
            dve_seen += KD
            pe.wait_ge(dve_evac, SEED + dve_seen)

            for c in range(2):
                last = pe.transpose(bank[4 + c][0:CW * KR, 0:P], ST[:, c, :], ident[:, :])
            last.then_inc(st_t, 1)
            for i, (t, n) in enumerate(TT):
                for q in range(KD // 4):
                    u = i * (KD // 4) + q
                    if u >= 4:
                        pe.wait_ge(x2_ready, u - 3)
                    for k in range(4 * q, 4 * q + 4):
                        last = pe.transpose(bank[u % 4][0:n, (k % 4) * P:(k % 4 + 1) * P], XNT[:, k, t:t + n], ident[:, :])
                    last.then_inc(x2_t, 1)
            pe.wait_ge(x2_ready, 3 * KD // 4)
            pe.wait_ge(xn2_ready, 3)
            for k in range(KD):
                if k >= 4:
                    pe.wait_ge(xn2t_ready, k - 3)
                for i, (t, n) in enumerate(TT):
                    last = pe.transpose(bank[k % 4][:, t:t + n], xntok[0:n, i, k * P:(k + 1) * P], ident[0:n, 0:n])
                last.then_inc(xn2_t, 1)
            pe.wait_ge(xn2t_ready, KD)
            pe.wait_ge(st_ready, 1)
            R = NG + NE
            for i, (t, n) in enumerate(TT):
                for k in range(KD):
                    last = pe.matmul(bank[4][0:n, i * R:(i + 1) * R], xn2t[:, k, t:t + n], wrt[:, k, :],
                                     start=(k == 0), stop=(k == KD - 1))
            last.then_inc(logits, 1)
            pe.wait_ge(chosen, 1)
            for i, (t, n) in enumerate(TT):
                for j in range(i + 1):
                    m = TT[j][1]
                    pe.matmul(bank[5][0:n, i * NE:(i + 1) * NE], (before if j == i else ones)[0:m, 0:n],
                              picked[0:m, j, :], start=(j == 0), stop=(j == i))
            for j, (_, m) in enumerate(TT):
                last = pe.matmul(bank[6][:, 0:NE], ones[0:m, :], picked[0:m, j, :], start=(j == 0), stop=(j == 2))
            last.then_inc(rank_mm, 1)

            pe.wait_ge(add2_ready, 1)
            pe.wait_ge(rounds_ready, 1)
            nr = pe.value_load(nrounds[0:1, 0:1], min_val=1, max_val=MAXR)

            def gather_transpose(p1):
                pe.wait_ge(rows_gathered, p1 * 16)
                for b in range(4):
                    for c in range(4):
                        k = 4 * b + c
                        last = pe.transpose(bank[b][:, c * P:(c + 1) * P], rows[:, k * P:(k + 1) * P], ident[:, :])
                last.then_inc(rows_t_done, 1)

            gather_transpose(1)
            with pe.Fori(0, nr * NPAIR) as p:
                for e in range(2):
                    if e == 0:
                        pe.wait_ge(xgt_ready, p + 1)
                    for u in range(4):
                        ru, c = 6 * e + u, u // 2
                        pe.wait_ge(w_rest, p * 12 + (ru + 1))
                        if u % 2 == 0:
                            pe.wait_ge(gu_copied, p * 4 + (2 * e + c + 1))
                        for k in range(KD // 2):
                            lhs = xs[:, (u % 2) * (KD // 2) + k, e, :]
                            for part in (w_high[ru % 2], w_low[ru % 4]):
                                last = pe.matmul(bank[4 + c][:, 0:DE], lhs, part[:, k * DE:(k + 1) * DE],
                                                 start=(u % 2 == 0 and k == 0 and part is w_high[ru % 2]),
                                                 stop=(u % 2 == 1 and k == KD // 2 - 1 and part is not w_high[ru % 2]))
                        last.then_inc(groups_done, 1)
                    if e == 1:
                        pe.wait_ge(y_out, p * 2 + 2)
                        gather_transpose(p + 2)
                    pe.wait_ge(h_act, p * 2 + (e + 1))
                    for c in range(2):
                        pe.wait_ge(gu_copied, p * 4 + (2 * e + c + 3))
                        for j in range(KE):
                            last = pe.matmul(bank[6][:, (c * KE + j) * CAP:(c * KE + j + 1) * CAP],
                                             gu[:, c, j * P:(j + 1) * P], add2[:, :], start=True, stop=True)
                    last.then_inc(gu_summed, 1)
                    pe.wait_ge(h_act, p * 2 + (e + 2))
                    if e == 0:
                        pe.wait_ge(y_out, p * 2 + 1)
                    else:
                        pe.wait_ge(xgt_ready, p + 2)
                    for u in range(2):
                        ru = 6 * e + 4 + u
                        pe.wait_ge(w_rest, p * 12 + (ru + 1))
                        for c in range(2):
                            for k in range(KE):
                                cols = slice(k * (DM // 2) + c * DE, k * (DM // 2) + (c + 1) * DE)
                                hh, hl = hs_high[:, k * CAP:(k + 1) * CAP], hs_low[:, k * CAP:(k + 1) * CAP]
                                dst = bank[2 * u + c][0:CAP, 0:DE]
                                pe.matmul(dst, hh, w_high[ru % 2][:, cols], start=(k == 0), stop=False)
                                pe.matmul(dst, hl, w_high[ru % 2][:, cols], start=False, stop=False)
                                last = pe.matmul(dst, hh, w_low[ru % 4][:, cols], start=False, stop=(k == KE - 1))
                        last.then_inc(groups_done, 1)

        @block.scalar
        def _(act):
            own = Steps(act, act_steps)

            def load_x(done):
                split = [(0, NM, P - NM), (P - NM, 0, P), (2 * P - NM, 0, PL)]
                act.dma_start(xtok[0:NM, 0, :], A["meta_tokens"]).then_inc(done, 16)
                for i, (r, p0, n) in enumerate(split):
                    act.dma_start(xtok[p0:p0 + n, i, :], A["x_prompt"][0, r:r + n, :]).then_inc(done, 16)
                act.dma_start(xtok[PL:NL, 2, :], A["x_sample"][0]).then_inc(done, 16)

            load_x(x_loaded)

            def rows_of(name, k):
                return A[name].rearrange("a (k f) -> (a k) f", k=k)
            r = 0
            for name, k in (("norm1_w", KD), ("norm2_w", KD), ("mlstm_norm_w", KD), ("conv_b", KR),
                            ("rg_a_b", KR), ("rg_x_b", KR), ("rg_lambda", KR)):
                act.dma_start(vstage[r:r + k, 0, :], rows_of(name, k)).then_inc(vec_loaded, 16)
                r += k
            act.dma_start(vstage[0:CW * KR, 1, :], A["conv_w"][0].rearrange("w (k f) -> (w k) f", k=KR)).then_inc(vec_loaded, 16)
            act.dma_start(vstage[CW * KR:VB_ROWS, 1, :], A["state_rglru_h"][0].rearrange("a (k f) -> (a k) f", k=KR)).then_inc(vec_loaded, 16)
            act.dma_start(vstage[0:VC_ROWS, 2, :], A["state_rglru_conv"][0, 0].rearrange("w (k f) -> (w k) f", k=KR)).then_inc(vec_loaded, 16)
            act.dma_start(wgif[:, :, :], w_in[:, :, C_GIF:C_GIF + 2 * NH]).then_inc(par_loaded, 16)
            act.dma_start(wrt[:, :, 0:NG], A["w_router_group"][0].rearrange("(k p) n -> p k n", p=P)).then_inc(par_loaded, 16)
            act.dma_start(wrt[:, :, NG:NG + NE], A["w_router_expert"][0].rearrange("(k p) n -> p k n", p=P)).then_inc(par_loaded, 16)
            act.dma_start(gates8[:, 2:4], A["b_gates"][0].rearrange("(c h) -> h c", h=NH), allow_slow_non_contiguous=True).then_inc(par_loaded, 16)
            act.dma_start(gates8[:, 0:1], A["state_mlstm_m"][0].rearrange("a h -> h a"), allow_slow_non_contiguous=True).then_inc(par_loaded, 16)
            act.dma_start(nst[:, 2 * NH:3 * NH], A["state_mlstm_n"][0, 0].rearrange("h k -> k h"), allow_slow_non_contiguous=True).then_inc(par_loaded, 16)

            act.wait_ge(x_loaded, 16 * 5)
            act.wait_ge(ss_init, 1)
            for i, (t, n) in enumerate(TT):
                act.activation(junk[0:n], xtok[0:n, i, :], ACT.Square, accum_out=small[0:n, i:i + 1]).then_inc(ss_done, 1)
                act.wait_ge(ss_done, i + 1)
            act.wait_ge(var_ready, 1)
            act.activation(small[:, 3:6], small[:, 3:6], ACT.Sqrt).then_inc(std_ready, 1)
            act.wait_ge(lam_abs, 1)
            act.activation(tmp[:, 0:KR], tmp[:, 0:KR], ACT.Exp, scale=-1.0).then_inc(lam_exp, 1)

            act.sem_inc(act_evac, SEED)
            act.sem_inc(gate_evac, SEED)
            act.wait_ge(dve_evac, SEED + 2 * KR)
            act.activation(XG[:, KR:2 * KR, :], XG[:, KR:2 * KR, :], ACT.Gelu_apprx_tanh).then_inc(gelu_done, 1)

            def group(g, first, dest):
                for m in range(2):
                    for jj in range(4 * m, 4 * m + 4):
                        act.wait_ge(groups_done, g * 8 + (G_QK + first * 8 + jj + 1))
                        act.activation(dest(g, jj), bank[jj % 4][:, 0:T], ACT.Copy).then_inc(act_evac, 1)
                    if m == 0:
                        act.wait_ge(group_done, g + (first + 1))
                    for j in range(GT):
                        act.wait_ge(gate_mm, g * (2 * GT) + (GATE_SEED + first * 2 * GT + m * GT + j + 1))
                        b0 = (V_AB, V_XB)[m] + first * GT + j
                        act.activation(RT[j] if m == 0 else AB[:, j, :], bank[4 + j % 4][:, 0:CONV], ACT.Sigmoid,
                                       bias=vec[:, bass.ds(g * GT + b0, 1)]).then_inc(gate_evac, 1)
                act.wait_ge(gated, g + (first + 1))
                act.wait_ge(gate_evac, g * (2 * GT) + (SEED + (first + 1) * 2 * GT))
                for j in range(GT):
                    c_ = CL[:, bass.ds(g * GT + (first * GT + j), 1)]
                    own.step(act.activation(AB[:, j, :], RT[j], ACT.Exp, scale=c_), beside=gelu_done)
                for j in range(GT):
                    c_ = CL[:, bass.ds(g * GT + (first * GT + j), 1)]
                    last = act.activation(RT[j], RT[j], ACT.Tanh, scale=c_)
                last.then_inc(a_ready, 1)
                act.wait_ge(sq_ready, g + (first + 1))
                for j in range(GT):
                    last = act.activation(RT[j], RT[j], ACT.Sqrt, scale=-1.0)
                last.then_inc(sqrt_done, 1)

            with act.Fori(0, 2) as g:
                own.enter(g, GT)
                group(g, 0, lambda g, jj: HB[:, jj, bass.ds(g * T, T)])
            own.leave(2)
            with act.Fori(0, 2) as g:
                own.enter(g, GT)
                group(g, 2, lambda g, jj: OG[:, bass.ds(g * 8 + jj, 1), :].rearrange("p a t -> p (a t)"))
            own.leave(2)

            act.wait_ge(z_abs, 1)
            act.activation(t0, t0, ACT.Exp, scale=-1.0).then_inc(z_exp, 1)
            act.wait_ge(mrow_ready, 1)
            act.activation(expnm[0:NH], t1, ACT.Exp, scale=-1.0)
            act.activation(wp[:, 0:TP], gg[:, 0:TP], ACT.Exp, bias=negM[0:NH, TP - 1:TP])
            act.activation(ws[:, TP:T], gg[:, TP:T], ACT.Exp, bias=negM[0:NH, T - 1:T])
            act.activation(gates8[:, 1:2], gates8[:, 0:1], ACT.Exp, bias=negM[0:NH, T - 1:T]).then_inc(row_exp, 1)
            act.wait_ge(act_evac, SEED + 8 * G)
            act.activation(OGf[:, :], OGf[:, :], ACT.Sigmoid).then_inc(og_ready, 1)

            act.wait_ge(gt_ready, 1)
            with act.Fori(0, NH // 2) as hp:
                for e in range(2):
                    h = hp * 2 + e
                    h1 = hp * 2 + (e + 1)

                    def merge_tile(j):
                        wait_apart(act, gt_ready, groups_done, hp * 8 + (G_MG + 4 * e + j + 1))
                        act.activation(HB[:, bass.ds(h, 1), j * T:(j + 1) * T].rearrange("p a t -> p (a t)"),
                                       bank[j][:, 0:T], ACT.Copy).then_inc(act_evac, 1)
                    act.wait_ge(pe_kt, h1)
                    act.activation(kh, HB[:, bass.ds(h, 1), T:2 * T].rearrange("p a t -> p (a t)"), ACT.Copy,
                                   scale=float(DQK) ** -0.5).then_inc(staged_a, 1)
                    act.wait_ge(staged_d, h1)
                    act.wait_ge(staged_a, h1)
                    merge_tile(0)
                    act.wait_ge(pe_scores, hp * 2 + (e + 2))
                    act.activation(es, bank[6][:, 0:T], ACT.Copy).then_inc(es_ready, 1)
                    act.wait_ge(d_ready, h1)
                    act.activation(small2[:, :], bank[5][:, TP:T], ACT.Exp,
                                   bias=hb16[:, bass.ds(h + NH, 1)]).then_inc(wi_ready, 1)
                    for i, (rows_, c, n, t) in enumerate(SC):
                        last = act.activation(dw[0:rows_, c:c + n], dw[0:rows_, c:c + n], ACT.Exp,
                                              bias=gtok[0:rows_, i, bass.ds(h, 1)])
                    last.then_inc(w_ready, 1)
                    merge_tile(1)
                    act.wait_ge(h_ready, h1)
                    act.activation(sq, hh, ACT.Square).then_inc(sq_h, 1)
                    merge_tile(2)
                    act.wait_ge(vr_ready, h1)
                    act.activation(rd, rd, ACT.Sqrt).then_inc(sr_ready, 1)
                    merge_tile(3)
            act.wait_ge(act_evac, SEED + 8 * G + 2 * KD)
            with act.Fori(0, NH) as h:
                mgb = HB[:, bass.ds(h, 1), 0:4 * T].rearrange("p a t -> p (a t)")
                act.activation(mgb, mgb, ACT.Sigmoid).then_inc(mg_ready, 1)

            act.wait_ge(head_done, NH)
            act.wait_ge(cn_stored, 32 * NH)
            act.wait_ge(pe_cn, NH + 1)
            load_x(xr_loaded)
            act.wait_ge(groups_done, G_OUT)
            act.dma_start(nb2, bcast(A["norm2_w"][0])).then_inc(nb_loaded, 16)
            act.dma_start(nbf, bcast(A["norm_f_w"])).then_inc(nb_loaded, 16)
            act.dma_start(brt[:, 0:NG], bcast(A["b_router_group"][0])).then_inc(nb_loaded, 16)
            act.dma_start(brt[:, NG:NG + NE], bcast(A["b_router_expert"][0])).then_inc(nb_loaded, 16)
            act.wait_ge(x2_ready, 3 * KD // 4)
            act.wait_ge(groups_done, G_MOE)
            for i, (t, n) in enumerate(TT):
                act.activation(junk2[0:n], xtok[0:n, i, :], ACT.Square, accum_out=small[0:n, 9 + i:10 + i]).then_inc(ss2_done, 1)
                act.wait_ge(ss2_done, i + 1)
            act.wait_ge(var2, 1)
            act.activation(small[:, 12:15], small[:, 12:15], ACT.Sqrt).then_inc(std2, 1)
            act.wait_ge(cols_e, 1)
            act.activation(gkey, gkey, ACT.Exp)
            act.activation(ex, ex, ACT.Exp).then_inc(exps_e, 1)

            act.sem_inc(gu_copied, 2)
            act.wait_ge(rounds_ready, 1)
            act.wait_ge(xn2_stored, 16 * 3)
            nr = act.value_load(nrounds[0:1, 0:1], min_val=1, max_val=MAXR)

            def split_weights(p, ru):
                b = ru % 4
                act.wait_ge(slot_full[b], (p * 3 + (ru // 4 + LOADS_MOE[b] + 1)) * 16)
                act.wait_ge(groups_done, p * 12 + (G_MOE + ru - 1))
                act.activation(w_high[ru % 2], w_raw[b], ACT.Copy).then_inc(w_split, 1)

            def split_rows(p1):
                act.wait_ge(rows_t_done, p1)
                for b in range(4):
                    act.activation(xs[:, 4 * b:4 * b + 4, :, 0:CAP],
                                   bank[b][:, :].rearrange("p (k e c) -> p k e c", k=4, e=2), ACT.Copy).then_inc(xs_high, 1)

            def copy_gu(p, e, c):
                act.wait_ge(groups_done, p * 12 + (G_MOE + 6 * e + 2 * c + 2))
                if c == 0:
                    act.wait_ge(gu_summed, p * 2 + (e + 1))
                act.activation(gu[:, c, :], bank[4 + c][:, 0:DE], ACT.Copy).then_inc(gu_copied, 1)

            act.sem_inc(gu_summed, 1)
            split_rows(1)
            split_weights(0, 0)
            with act.Fori(0, nr * NPAIR) as p:
                for e in range(2):
                    for u in range(1, 4):
                        split_weights(p, 6 * e + u)
                    copy_gu(p, e, 0)
                    split_weights(p, 6 * e + 4)
                    copy_gu(p, e, 1)
                    act.wait_ge(gu_summed, p * 2 + (e + 2))
                    act.wait_ge(h_act, p * 2 + (e + 1))
                    act.activation(sg, bank[6][:, 0:HC], ACT.Silu).then_inc(silu_done, 1)
                    if e == 1:
                        split_rows(p + 2)
                    split_weights(p, 6 * e + 5)
                    split_weights(p, 6 * e + 6)

            act.wait_ge(fin_ss, 1)
            for i, (t, n) in enumerate(TT):
                act.activation(y1[0:n, i, :], xtok[0:n, i, :], ACT.Square, accum_out=small[0:n, 18 + i:19 + i]).then_inc(fin_sq, 1)
            act.wait_ge(fin_var, 1)
            act.activation(small[:, 21:24], small[:, 21:24], ACT.Sqrt).then_inc(fin_std, 1)

        @block.vector
        def _(v):
            own = Steps(v, dve_steps)
            step = own.step

            def log1p(e, s, s2, p):
                step(v.tensor_scalar(s, e, 2.0, None, ALU.add))
                step(v.reciprocal(s, s))
                step(v.tensor_tensor(s, s, e, ALU.mult))
                step(v.tensor_tensor(s2, s, s, ALU.mult))
                step(v.tensor_scalar(p, s2, 1.0 / 15, None, ALU.mult))
                for c in (13, 11, 9, 7, 5, 3):
                    step(v.scalar_tensor_tensor(out=p, in0=p, scalar=1.0 / c, in1=s2, op0=ALU.add, op1=ALU.mult))
                step(v.scalar_tensor_tensor(out=p, in0=p, scalar=1.0, in1=s, op0=ALU.add, op1=ALU.mult))
                step(v.tensor_scalar(p, p, 2.0, None, ALU.mult))

            def root_mean(a, b, n_, ready, rooted):
                v.tensor_scalar(small[:, b:b + 3], small[:, a:a + 3], 1.0 / n_, EPS, ALU.mult, ALU.add).then_inc(ready, 1)
                v.wait_ge(rooted, 1)

            v.sem_inc(cn_ready, 1)
            v.memset(small[:, :], 1.0).then_inc(ss_init, 1)
            v.wait_ge(vec_transposed, 1)
            for c, n in ((0, P), (1, VB_ROWS), (2, VC_ROWS)):
                last = v.tensor_copy(vec[:, c * P:c * P + n], bank[4][:, c * P:c * P + n])
            last.then_inc(vec_ready, 1)
            v.wait_ge(ss_done, 3)
            root_mean(0, 3, DM, var_ready, std_ready)
            step(v.reciprocal(small[:, 6:9], small[:, 3:6]))
            for i, (t, n) in enumerate(TT):
                v.tensor_scalar(xntok[0:n, i, :], xtok[0:n, i, :], small[0:n, 6 + i:7 + i], None, ALU.mult).then_inc(xn_ready, 1)
            v.wait_ge(vec_ready, 1)
            lam = vec[:, V_LM:V_LM + KR]
            v.scalar_tensor_tensor(out=tmp[:, 0:KR], in0=lam, scalar=-1.0, in1=lam, op0=ALU.mult, op1=ALU.max).then_inc(lam_abs, 1)
            for k in range(KD):
                v.wait_ge(x_transposed, k + 1)
                v.tensor_scalar(XNT[:, k, :], bank[k % 4][:, 0:T], vec[:, V_N1 + k:V_N1 + k + 1], None, ALU.mult).then_inc(xnt_ready, 1)
            v.wait_ge(lam_exp, 1)
            log1p(tmp[:, 0:KR], tmp[:, KR:2 * KR], tmp[:, 2 * KR:3 * KR], CL[:, :])
            step(v.tensor_scalar(tmp[:, 0:KR], lam, -1.0, 0.0, ALU.mult, ALU.max))
            step(v.tensor_tensor(CL[:, :], CL[:, :], tmp[:, 0:KR], ALU.add))
            step(v.tensor_scalar(CL[:, :], CL[:, :], -8.0, None, ALU.mult))

            v.sem_inc(dve_evac, SEED)
            v.memset(XG[:, :, 0:CW - 1], 0.0)
            step(v.memset(XG[:, :, S0:S0 + CW - 1], 0.0))
            step(v.tensor_copy(XG[:, 0:KR, S0:S0 + CW - 1],
                               vec[:, V_CS:V_CS + VC_ROWS].rearrange("p (w k) -> p k w", k=KR)))
            with v.Fori(0, 2 * KR // 8) as i:
                for jj in range(8):
                    v.wait_ge(groups_done, i * 8 + (jj + 1))
                    dst = XG[:, bass.ds(i * 8 + jj, 1), :].rearrange("p a t -> p (a t)")
                    v.tensor_copy(dst[:, CW - 1:CW - 1 + TP], bank[jj % 4][:, 0:TP])
                    v.tensor_copy(dst[:, S0 + CW - 1:PADDED], bank[jj % 4][:, TP:T]).then_inc(dve_evac, 1)

            v.wait_ge(dve_evac, SEED + 2 * KR)
            for c, first in ((0, TP), (1, PADDED - (CW - 1))):
                last = v.tensor_copy(ST[:, c, KR:].rearrange("p (w k) -> p k w", k=KR), XG[:, 0:KR, first:first + CW - 1])
            last.then_inc(states_saved, 1)
            v.wait_ge(states_saved, 1)
            with v.Fori(0, KR) as k:
                own.enter(k, CW - 1)
                xr = XG[:, bass.ds(k, 1), :].rearrange("p a t -> p (a t)")

                def tap(w):
                    return vec[:, bass.ds(k + (V_CW + w * KR), 1)]
                step(v.tensor_scalar(tmp, xr[:, 0:CONV], tap(0), vec[:, bass.ds(k + V_CB, 1)], ALU.mult, ALU.add))
                for w in range(1, CW - 1):
                    step(v.scalar_tensor_tensor(out=tmp, in0=xr[:, w:w + CONV], scalar=tap(w), in1=tmp, op0=ALU.mult, op1=ALU.add))
                v.scalar_tensor_tensor(out=xr[:, 0:CONV], in0=xr[:, CW - 1:CW - 1 + CONV], scalar=tap(CW - 1), in1=tmp,
                                       op0=ALU.mult, op1=ALU.add).then_inc(conv_done, 1)
                v.wait_ge(conv_done, k + 1)
            own.leave(KR)
            v.wait_ge(conv_done, KR)

            v.sem_inc(group_done, 1)
            v.wait_ge(gelu_done, 1)
            with v.Fori(0, G) as g:
                own.enter(g, 6 * GT + 1)
                XC = XG[:, bass.ds(g * GT, GT), :]
                YR = XG[:, bass.ds(g * GT + KR, GT), :]
                v.wait_ge(gate_evac, g * (2 * GT) + (SEED + 2 * GT))
                v.tensor_tensor(XC[:, :, 0:CONV], XC[:, :, 0:CONV], AB[:, :, :], ALU.mult).then_inc(gated, 1)
                v.wait_ge(a_ready, g + 1)
                for j in range(GT):
                    step(v.tensor_tensor(tmp, AB[:, j, :], AB[:, j, :], ALU.mult))
                    last = v.scalar_tensor_tensor(out=RT[j], in0=tmp, scalar=1.0, in1=RT[j], op0=ALU.add, op1=ALU.mult)
                    if j < GT - 1:
                        step(last)
                last.then_inc(sq_ready, 1)
                v.wait_ge(sqrt_done, g + 1)
                for j in range(GT):
                    step(v.tensor_tensor(XC[:, j, 0:CONV], XC[:, j, 0:CONV], RT[j], ALU.mult))
                step(v.memset(AB[:, :, S0 - 1:S0], 0.0))
                step(v.tensor_copy(XC[:, :, S0 - 1:S0], vec[:, bass.ds(g * GT + V_H0, GT)].rearrange("p (k a) -> p k a", a=1)))
                for j in range(GT):
                    step(v.tensor_tensor_scan(RT[j], AB[:, j, :], XC[:, j, 0:CONV], 0.0, ALU.mult, ALU.add))
                for j in range(GT):
                    for c, col in ((0, TP - 1), (1, CONV - 1)):
                        v.tensor_copy(ST[:, c, bass.ds(g * GT + j, 1)], RT[j][:, col:col + 1])
                    step(v.tensor_tensor(YR[:, j, 0:TP], YR[:, j, CW - 1:CW - 1 + TP], RT[j][:, 0:TP], ALU.mult))
                for j in range(GT):
                    step(v.tensor_tensor(YR[:, j, TP:T], YR[:, j, S0 + CW - 1:PADDED], RT[j][:, S0:CONV], ALU.mult))
                v.sem_inc(group_done, 1)
            own.leave(G)

            v.wait_ge(gif_done, 2)
            v.tensor_scalar(li, bank[4][0:NH, 0:T], gates8[:, 2:3], None, ALU.add)
            step(v.tensor_scalar(lf, bank[5][0:NH, 0:T], gates8[:, 3:4], None, ALU.add))
            v.scalar_tensor_tensor(out=t0, in0=lf, scalar=-1.0, in1=lf, op0=ALU.mult, op1=ALU.max).then_inc(z_abs, 1)
            v.wait_ge(z_exp, 1)
            log1p(t0, bc, gg, wp)
            step(v.scalar_tensor_tensor(out=lf, in0=lf, scalar=0.0, in1=wp, op0=ALU.min, op1=ALU.subtract))
            step(v.memset(t1, 1.0))
            v.tensor_tensor_scan(bc[:, 0:TP], t1[:, 0:TP], lf[:, 0:TP], 0.0, ALU.mult, ALU.add)
            step(v.tensor_tensor_scan(bc[:, TP:T], t1[:, TP:T], lf[:, TP:T], 0.0, ALU.mult, ALU.add))
            step(v.tensor_tensor(gg, li, bc, ALU.subtract))
            v.tensor_tensor_scan(t0[:, 0:TP], gg[:, 0:TP], gg[:, 0:TP], 0.0, ALU.max, ALU.max)
            step(v.tensor_tensor_scan(t0[:, TP:T], gg[:, TP:T], gg[:, TP:T], gates8[:, 0:1], ALU.max, ALU.max))
            v.tensor_scalar(negM[0:NH], t0, -1.0, None, ALU.mult)
            step(v.tensor_tensor(t1, bc, t0, ALU.add))
            v.tensor_copy(gates8[:, 4:5], t1[:, TP - 1:TP])
            v.tensor_copy(gates8[:, 5:6], t1[:, T - 1:T])
            v.memset(wp, 0.0)
            v.memset(ws, 0.0).then_inc(mrow_ready, 1)
            v.wait_ge(row_exp, 1)
            v.tensor_scalar(diag8[:, 0:NH], ident[0:NH, 0:NH], gates8[:, 1:2], None, ALU.mult)
            v.tensor_scalar(diag8[:, NH:2 * NH], ident[0:NH, 0:NH], gates8[:, 0:1], None, ALU.mult).then_inc(rows_t, 1)

            with v.Fori(0, 2) as i:
                for b in range(4):
                    for c, (t, n) in enumerate(TT):
                        jj = 3 * b + c
                        v.wait_ge(groups_done, i * 12 + (G_V + jj + 1))
                        dst = HB[0:n, bass.ds(i * 4 + b, 1), HV0 + c * DV:HV0 + (c + 1) * DV].rearrange("p a t -> p (a t)")
                        v.tensor_copy(dst, bank[jj % 4][0:n, 0:DV]).then_inc(dve_evac, 1)
            v.wait_ge(gt_mm, 1)
            for i, (t, n) in enumerate(TT):
                v.tensor_copy(gtok[0:n, i, :], bank[6][0:n, i * 3 * NH:(i + 1) * 3 * NH])
            v.tensor_copy(hb16[:, :], bank[7][:, 0:2 * NH]).then_inc(gt_ready, 1)
            v.wait_ge(gt_ready, 1)
            v.wait_ge(og_ready, 1)
            v.wait_ge(dve_evac, SEED + 2 * KR + 24)

            with v.Fori(0, NH) as h:
                own.enter(h, 8)
                h1 = h + 1

                def col(a, c0_, n=P):
                    return a[0:n, bass.ds(h + c0_, 1)]
                v.wait_ge(pe_scores, h1)
                v.wait_ge(pe_ss, h1)
                v.wait_ge(pe_cn, h1)
                v.tensor_scalar(selM[0:NH], negM[0:NH], ident[0:NH, bass.ds(h, 1)], None, ALU.mult)
                v.tensor_scalar(selE[0:NH], expnm[0:NH], ident[0:NH, bass.ds(h, 1)], None, ALU.mult)
                v.tensor_scalar(n0b, ones[:, :], col(nst, 2 * NH), None, ALU.mult)
                hb = HB[:, bass.ds(h, 1), :].rearrange("p a t -> p (a t)")
                v.tensor_copy(vh[:, 0:2 * DV], hb[:, HV0:HV0 + 2 * DV])
                v.tensor_copy(vh[0:NL, 2 * DV:3 * DV], hb[0:NL, HV0 + 2 * DV:HV0 + 3 * DV])
                v.tensor_copy(qh, hb[:, 0:T]).then_inc(staged_d, 1)
                v.wait_ge(pe_scores, h + 2)
                v.tensor_tensor(dw[:, 0:TP], bank[5][:, 0:TP], tri[:, 0:TP], ALU.add)
                v.tensor_tensor(dw[:, TP:2 * TP - P], bank[5][:, P:TP], tri[:, 0:TP - P], ALU.add)
                c = SC[2][1]
                v.tensor_tensor(dw[0:NL, c:c + NL], bank[5][0:NL, 2 * P:T], trl[:, :], ALU.add).then_inc(d_ready, 1)
                v.wait_ge(staged_d, h1)
                v.wait_ge(wi_ready, h1)
                step(v.tensor_tensor(small2[:, :], small2[:, :], qh[:, TP:T], ALU.mult))
                v.wait_ge(w_ready, h1)
                v.tensor_tensor(dw[:, 0:c], dw[:, 0:c], bank[4][:, 0:c], ALU.mult)
                v.tensor_tensor(dw[0:NL, c:c + NL], dw[0:NL, c:c + NL], bank[4][0:NL, c:c + NL], ALU.mult).then_inc(sw_ready, 1)
                v.wait_ge(pe_num, h + 2)
                v.wait_ge(es_ready, h1)
                step(v.scalar_tensor_tensor(out=rd, in0=bank[5][:, 0:T], scalar=-1.0, in1=es, op0=ALU.mult, op1=ALU.max))
                step(v.tensor_tensor(rd, rd, bank[5][:, 0:T], ALU.max))
                step(v.reciprocal(rd, rd))
                v.tensor_tensor(hh[:, 0:T], bank[6][:, 0:T], rd, ALU.mult)
                v.tensor_tensor(hh[:, T:2 * T], bank[7][:, 0:T], rd, ALU.mult).then_inc(h_ready, 1)
                v.wait_ge(pe_kt, h + 2)
                for i, (t, n) in enumerate(TT):
                    v.tensor_scalar(kp[0:n, i * DQK:(i + 1) * DQK], bank[4][0:n, i * P:i * P + DQK],
                                    gtok[0:n, i, bass.ds(h + NH, 1)], None, ALU.mult)
                v.tensor_scalar(ks[0:NL], bank[4][0:NL, 2 * P:2 * P + DQK],
                                gtok[0:NL, 2, bass.ds(h + 2 * NH, 1)], None, ALU.mult).then_inc(kp_ready, 1)
                v.wait_ge(pe_ss, h + 2)
                v.wait_ge(h_ready, h1)
                v.tensor_scalar(rd, bank[5][:, 0:T], 1.0 / DV, EPS, ALU.mult, ALU.add).then_inc(vr_ready, 1)
                v.wait_ge(sr_ready, h1)
                step(v.reciprocal(rd, rd))
                for c in range(2):
                    last = v.scalar_tensor_tensor(out=hh[:, c * T:(c + 1) * T], in0=hh[:, c * T:(c + 1) * T],
                                                  scalar=vec[:, bass.ds(h * 2 + (V_MN + c), 1)], in1=rd, op0=ALU.mult, op1=ALU.mult)
                step(last)
                og = OG[:, bass.ds(h * 2, 2), :].rearrange("p a t -> p (a t)")
                v.tensor_tensor(og, og, hh, ALU.mult).then_inc(head_done, 1)
                v.wait_ge(pe_cn, h + 2)
                v.tensor_copy(cn[:, 0:DV], bank[6][:, 0:DV])
                step(v.tensor_copy(nst[:, bass.ds(h, 1)], bank[7][:, 0:1]))
                step(v.scalar_tensor_tensor(out=nst[:, bass.ds(h + NH, 1)], in0=col(nst, 2 * NH), scalar=col(hb16, 0),
                                            in1=bank[7][:, 1:2], op0=ALU.mult, op1=ALU.add))
                v.scalar_tensor_tensor(out=cn[:, DV:2 * DV], in0=c0, scalar=col(hb16, 0), in1=bank[6][:, DV:2 * DV],
                                       op0=ALU.mult, op1=ALU.add).then_inc(cn_ready, 1)
            own.leave(NH)

            with v.Fori(0, KD // 4) as i:
                v.wait_ge(mg_ready, i + 1)
                for j in range(4):
                    v.wait_ge(groups_done, i * 4 + (G_PR + j + 1))
                    m = HB[:, bass.ds(i, 1), j * T:(j + 1) * T].rearrange("p a t -> p (a t)")
                    v.tensor_tensor(m, m, bank[j][:, 0:T], ALU.mult).then_inc(dve_evac, 1)
            v.wait_ge(dve_evac, SEED + 2 * KR + 24 + KD)
            with v.Fori(0, KD // 8) as i:
                own.enter(i, 8)
                for jj in range(8):
                    b, j = jj // 4, jj % 4
                    v.wait_ge(mg_ready, i * 2 + (KD // 4 + b + 1))
                    v.wait_ge(groups_done, i * 8 + (G_PM + jj + 1))
                    m = HB[:, bass.ds(i * 2 + (KD // 4 + b), 1), j * T:(j + 1) * T].rearrange("p a t -> p (a t)")
                    r_ = HB[:, bass.ds(i * 2 + b, 1), j * T:(j + 1) * T].rearrange("p a t -> p (a t)")
                    step(v.tensor_tensor(m, m, bank[j][:, 0:T], ALU.mult))
                    v.tensor_tensor(r_, r_, m, ALU.add).then_inc(dve_evac, 1)
            own.leave(KD // 8)
            with v.Fori(0, KD // 8) as i:
                for jj in range(8):
                    v.wait_ge(groups_done, i * 8 + (G_OUT + jj + 1))
                    v.tensor_copy(XNT[:, bass.ds(i * 8 + jj, 1), :].rearrange("p a t -> p (a t)"),
                                  bank[jj % 4][:, 0:T]).then_inc(dve_evac, 1)
            v.wait_ge(st_t, 1)
            for c in range(2):
                last = v.tensor_copy(vec[0:CW * KR, c * P:(c + 1) * P], bank[4 + c][0:CW * KR, 0:P])
            last.then_inc(st_ready, 1)
            v.wait_ge(xr_loaded, 16 * 5)
            for i, (t, n) in enumerate(TT):
                for q in range(KD // 4):
                    u = i * (KD // 4) + q
                    v.wait_ge(x2_t, u + 1)
                    c = slice(q * 4 * P, (q + 1) * 4 * P)
                    v.tensor_tensor(xtok[0:n, i, c], xtok[0:n, i, c], bank[u % 4][0:n, :], ALU.add).then_inc(x2_ready, 1)
            v.wait_ge(ss2_done, 3)
            root_mean(9, 12, DM, var2, std2)
            step(v.reciprocal(small[:, 15:18], small[:, 12:15]))
            v.wait_ge(nb_loaded, 16 * 4)
            for i, (t, n) in enumerate(TT):
                v.scalar_tensor_tensor(out=xntok[0:n, i, :], in0=xtok[0:n, i, :], scalar=small[0:n, 15 + i:16 + i],
                                       in1=nb2[0:n], op0=ALU.mult, op1=ALU.mult).then_inc(xn2_ready, 1)
            for k in range(KD):
                v.wait_ge(xn2_t, k + 1)
                v.tensor_copy(xn2t[:, k, :], bank[k % 4][:, 0:T]).then_inc(xn2t_ready, 1)

            v.memset(gl, 0.0)
            v.memset(el, 0.0)
            step(v.memset(rk, 0.0))
            v.wait_ge(logits, 1)
            R = NG + NE
            for i, (t, n) in enumerate(TT):
                v.tensor_tensor(gl[0:n, i, :], bank[4][0:n, i * R:i * R + NG], brt[0:n, 0:NG], ALU.add)
                last = v.tensor_tensor(el[0:n, i, :], bank[4][0:n, i * R + NG:(i + 1) * R], brt[0:n, NG:R], ALU.add)
            step(last)

            def wide_(a, n):
                return a.broadcast_to([P, 3, n])

            def first_max(x, key, mx, oh):
                step(v.tensor_reduce(mx, x, AX.X, ALU.max))
                step(v.tensor_tensor(key, x, wide_(mx, NG), ALU.is_equal))
                kj = kc[:, NE:NE + EG].rearrange("p (a j) -> p a j", a=1).broadcast_to([P, 3, EG])
                step(v.tensor_tensor(key, key, kj, ALU.mult))
                step(v.tensor_reduce(kmx, key, AX.X, ALU.max))
                step(v.tensor_tensor(oh, key, wide_(kmx, NG), ALU.is_equal))
            first_max(gl, gkey, gmx, goh)
            step(v.tensor_tensor(gkey, gl, wide_(gmx, NG), ALU.subtract))
            pg = prod.rearrange("p a (g j) -> p (a g) j", g=NG)
            step(v.tensor_tensor(pg, el.rearrange("p a (g j) -> p (a g) j", g=NG),
                                 goh.rearrange("p a (g o) -> p (a g) o", o=1).broadcast_to([P, 3 * NG, EG]), ALU.mult))
            step(v.tensor_reduce(ein, prod.rearrange("p a (g j) -> p a j g", g=NG), AX.X, ALU.add))
            first_max(ein, ekey, v1, o1)
            step(v.scalar_tensor_tensor(out=e2, in0=o1, scalar=NEG, in1=ein, op0=ALU.mult, op1=ALU.add))
            first_max(e2, ekey, v2, o2)
            v.tensor_tensor(ex, v2, v1, ALU.subtract).then_inc(cols_e, 1)
            for E_, o_ in ((E1, o1), (E2, o2)):
                for i in range(3):
                    last = v.tensor_tensor(E_[:, i, :].rearrange("p (g j) -> p g j", g=NG),
                                           goh[:, i, :].rearrange("p (g o) -> p g o", o=1).broadcast_to([P, NG, EG]),
                                           o_[:, i, :].rearrange("p (o j) -> p o j", o=1).broadcast_to([P, NG, EG]), ALU.mult)
            step(last)
            v.tensor_tensor(picked, E1, E2, ALU.add).then_inc(chosen, 1)
            v.wait_ge(exps_e, 1)
            step(v.tensor_reduce(gw, gkey, AX.X, ALU.add))
            step(v.tensor_scalar(w1, ex, 1.0, None, ALU.add))
            step(v.tensor_tensor(w1, w1, gw, ALU.mult))
            step(v.reciprocal(w1, w1))
            step(v.tensor_tensor(w2, ex, w1, ALU.mult))
            v.wait_ge(rank_mm, 1)
            for i, (t, n) in enumerate(TT):
                last = v.tensor_copy(rk[0:n, i, :], bank[5][0:n, i * NE:(i + 1) * NE])
            step(last)
            step(v.tensor_tensor(sl, rk, kc[:, 0:NE].rearrange("p (a j) -> p a j", a=1).broadcast_to([P, 3, NE]), ALU.add))
            for m in range(1, MAXR):
                step(v.tensor_scalar(slt, rk, float(m * CAP), float(ROUND_ROWS - CAP), ALU.is_ge, ALU.mult))
                step(v.tensor_tensor(sl, sl, slt, ALU.add))
            for c, E_ in enumerate((E1, E2)):
                step(v.tensor_tensor(slt, E_, sl, ALU.mult))
                step(v.tensor_reduce(slf[:, :, c:c + 1], slt, AX.X, ALU.add))
            step(v.tensor_copy(slot_i[:, :, :], slf.rearrange("p a c -> p c a")))
            step(v.tensor_reduce(cmx[:, 0:1], bank[6][:, 0:NE], AX.X, ALU.max))
            step(v.memset(cmx[:, 1:2], 1.0))
            for m in range(1, MAXR):
                step(v.scalar_tensor_tensor(out=cmx[:, 1:2], in0=cmx[:, 0:1], scalar=float(m * CAP), in1=cmx[:, 1:2],
                                            op0=ALU.is_gt, op1=ALU.add))
            v.tensor_copy(nrounds[:, :], cmx[:, 1:2]).then_inc(rounds_ready, 1)

            v.sem_inc(h_act, 1)
            v.sem_inc(y_out, 1)
            v.wait_ge(rounds_ready, 1)
            nr = v.value_load(nrounds[0:1, 0:1], min_val=1, max_val=MAXR)

            def rest_of_weights(p, ru):
                v.wait_ge(w_split, p * 12 + (ru + 1))
                v.tensor_tensor(w_low[ru % 4], w_raw[ru % 4], w_high[ru % 2].bitcast(F32), ALU.subtract).then_inc(w_rest, 1)

            def rest_of_rows(p):
                for b in range(4):
                    v.wait_ge(xs_high, p * 4 + (b + 1))
                    last = v.tensor_tensor(xs[:, 4 * b:4 * b + 4, :, CAP:2 * CAP],
                                           bank[b][:, :].rearrange("p (k e c) -> p k e c", k=4, e=2),
                                           xs[:, 4 * b:4 * b + 4, :, 0:CAP].bitcast(F32), ALU.subtract)
                last.then_inc(xgt_ready, 1)

            for b in range(4):
                v.wait_ge(xs_high, b + 1)
                last = v.tensor_tensor(xs[:, 4 * b:4 * b + 4, :, CAP:2 * CAP],
                                       bank[b][:, :].rearrange("p (k e c) -> p k e c", k=4, e=2),
                                       xs[:, 4 * b:4 * b + 4, :, 0:CAP].bitcast(F32), ALU.subtract)
            last.then_inc(xgt_ready, 1)
            v.wait_ge(w_split, 1)
            v.tensor_tensor(w_low[0], w_raw[0], w_high[0].bitcast(F32), ALU.subtract).then_inc(w_rest, 1)
            with v.Fori(0, nr * NPAIR) as p:
                for e in range(2):
                    for u in range(1, 5):
                        rest_of_weights(p, 6 * e + u)
                    v.wait_ge(silu_done, p * 2 + (e + 1))
                    v.tensor_tensor(hf, sg, bank[6][:, HC:2 * HC], ALU.mult).then_inc(h_steps, 1)
                    v.wait_ge(h_steps, p * 4 + (2 * e + 1))
                    v.tensor_copy(hs_high, hf).then_inc(h_steps, 1)
                    v.wait_ge(h_steps, p * 4 + (2 * e + 2))
                    v.tensor_tensor(hs_low, hf, hs_high.bitcast(F32), ALU.subtract).then_inc(h_act, 1)
                    if e == 1:
                        rest_of_rows(p + 1)
                    rest_of_weights(p, 6 * e + 5)
                    rest_of_weights(p, 6 * e + 6)
                    v.wait_ge(groups_done, p * 12 + (G_MOE + 6 * e + 6))
                    if e == 0:
                        v.wait_ge(y_free, p + 1)
                    for b in range(4):
                        last = v.tensor_copy(ysb[0:CAP, e, b * DE:(b + 1) * DE], bank[b][0:CAP, 0:DE])
                    last.then_inc(y_out, 1)

            v.wait_ge(y_loaded, 16 * 6)
            for i, (t, n) in enumerate(TT):
                step(v.scalar_tensor_tensor(out=xtok[0:n, i, :], in0=y1[0:n, i, :], scalar=w1[0:n, i, :],
                                            in1=xtok[0:n, i, :], op0=ALU.mult, op1=ALU.add))
            for i, (t, n) in enumerate(TT):
                last = v.scalar_tensor_tensor(out=xtok[0:n, i, :], in0=y2[0:n, i, :], scalar=w2[0:n, i, :],
                                              in1=xtok[0:n, i, :], op0=ALU.mult, op1=ALU.add)
            last.then_inc(fin_ss, 1)
            v.wait_ge(fin_sq, 3)
            root_mean(18, 21, DM, fin_var, fin_std)
            step(v.reciprocal(small[:, 0:3], small[:, 21:24]))
            for i, (t, n) in enumerate(TT):
                v.scalar_tensor_tensor(out=xtok[0:n, i, :], in0=xtok[0:n, i, :], scalar=small[0:n, i:i + 1],
                                       in1=nbf[0:n], op0=ALU.mult, op1=ALU.mult).then_inc(fin_out, 1)

        @block.gpsimd
        def _(pool):
            own = Steps(pool, pool_steps)
            step = own.step
            pool.memset(ones[:, :], 1.0)
            pool.memset(zeros_i[:, :], 0)
            for e in range(NE):
                pool.memset(kc[:, e:e + 1], float(e * CAP))
            for j in range(EG):
                pool.memset(kc[:, NE + j:NE + j + 1], float(EG - j))
            pool.memset(tri[:, :], 0.0)
            pool.memset(trl[:, :], 0.0)
            step(pool.memset(ident[:, :], 0.0))
            pool.affine_select(out=before[:, :], in_=ones[:, :], compare_op=ALU.is_gt, fill=0.0, base=0,
                               pattern=[[1, P]], channel_multiplier=-1)
            pool.affine_select(out=tri[:, :], in_=tri[:, :], compare_op=ALU.is_ge, fill=NEG, base=0,
                               pattern=[[1, TP]], channel_multiplier=-1)
            step(pool.affine_select(out=trl[:, :], in_=trl[:, :], compare_op=ALU.is_ge, fill=NEG, base=0,
                                    pattern=[[1, NL]], channel_multiplier=-1))
            step(pool.memset(trl[0:PL, PL:NL], NEG))
            pool.iota(tokid[:, :], pattern=[[P, 3]], base=0, channel_multiplier=1)
            pool.affine_select(out=ident[:, :], in_=ident[:, :], compare_op=ALU.not_equal, fill=1.0, base=0,
                               pattern=[[-1, P]], channel_multiplier=1).then_inc(consts_ready, 1)
            pool.wait_ge(consts_ready, 1)
            pool.dma_start(slot_token.rearrange("(p c) o -> p (c o)", p=P), zeros_i[:, :]).then_inc(zeroed, 16)

            pool.wait_ge(vec_ready, 1)
            pool.wait_ge(ss_done, 3)
            for m in range(2):
                for i in range(GT):
                    last = pool.memset(bd[m][i], 0.0)
            step(last)
            with pool.Fori(0, G) as g:
                for m, name in enumerate(("rg_a_w", "rg_x_w")):
                    wait_apart(pool, consts_ready, gate_mm, g * (2 * GT) + (GATE_SEED + m * GT - GT))
                    for b, r, n, i, p0 in PIECES:
                        c = RB * b - (i - 1) * P
                        pool.dma_start(bd[m][i][p0:p0 + n, c:c + RB],
                                       A[name][0, bass.ds(g * BG + b, 1), r:r + n, :].rearrange("a r c -> (a r) c")).then_inc(bd_loaded[m], 16)
            C0 = A["state_mlstm_C"][0, 0]
            pool.wait_ge(gt_ready, 1)
            pool.dma_start(O["p_m"][0].rearrange("a h -> h a"), gates8[:, 4:5], allow_slow_non_contiguous=True).then_inc(out_stored, 16)
            pool.dma_start(O["s_m"][0].rearrange("a h -> h a"), gates8[:, 5:6], allow_slow_non_contiguous=True).then_inc(out_stored, 16)
            with pool.Fori(0, NH) as h:
                pool.wait_ge(cn_ready, h + 1)
                pool.dma_start(c0, C0[bass.ds(h, 1), :, :].rearrange("a k v -> (a k) v")).then_inc(c0_loaded, 16)
                wait_apart(pool, gt_ready, cn_ready, h + 2)
                pool.dma_start(O["p_C"][0, 0][bass.ds(h, 1), :, :].rearrange("a k v -> (a k) v"), cn[:, 0:DV]).then_inc(cn_stored, 16)
                pool.dma_start(O["s_C"][0, 0][bass.ds(h, 1), :, :].rearrange("a k v -> (a k) v"), cn[:, DV:2 * DV]).then_inc(cn_stored, 16)
                pool.wait_ge(cn_stored, h * 32 + 32)
            pool.dma_start(O["p_n"][0, 0].rearrange("h k -> k h"), nst[:, 0:NH], allow_slow_non_contiguous=True).then_inc(out_stored, 16)
            pool.dma_start(O["s_n"][0, 0].rearrange("h k -> k h"), nst[:, NH:2 * NH], allow_slow_non_contiguous=True).then_inc(out_stored, 16)
            pool.wait_ge(st_ready, 1)
            for c, s_ in enumerate("ps"):
                pool.dma_start(O[s_ + "_h"][0].rearrange("a (k f) -> (a k) f", k=KR), vec[0:KR, c * P:(c + 1) * P]).then_inc(out_stored, 16)
                pool.dma_start(O[s_ + "_conv"][0, 0].rearrange("w (k f) -> (w k) f", k=KR),
                               vec[KR:CW * KR, c * P:(c + 1) * P]).then_inc(out_stored, 16)
            pool.wait_ge(xn2_ready, 3)
            for i, (t, n) in enumerate(TT):
                pool.dma_start(xn2_rows[t:t + n, :], xntok[0:n, i, :]).then_inc(xn2_stored, 16)
            pool.wait_ge(zeroed, 16)
            pool.wait_ge(rounds_ready, 1)
            pool.tensor_tensor(add2[:, :], ident[:, 0:CAP], ident[:, CAP:P], ALU.add).then_inc(add2_ready, 1)
            for c in range(2):
                for i, (t, n) in enumerate(TT):
                    pool.indirect_dma_start(out=slot_token[:, :], out_offset=bass.IndirectOffsetOnAxis(ap=slot_i[0:n, c, i:i + 1], axis=0),
                                            in_=tokid[0:n, i:i + 1], in_offset=None).then_inc(perm_written, 16)
            pool.wait_ge(perm_written, 16 * 6)
            pool.wait_ge(xn2_stored, 16 * 3)
            nr = pool.value_load(nrounds[0:1, 0:1], min_val=1, max_val=MAXR)
            with pool.If(nr > 1):
                step(pool.memset(HBf[:, 2 * DM:3 * DM], 0.0))
                with pool.Fori(0, (SLOTS - ROUND_ROWS) // P) as k:
                    pool.dma_start(slot_out[bass.ds(k * P + ROUND_ROWS, P), :], HBf[:, 2 * DM:3 * DM]).then_inc(rest_zeroed, 16)
                pool.wait_ge(rest_zeroed, (SLOTS - ROUND_ROWS) // P * 16)
            with pool.Else():
                pool.nop()

            def gather(p, p1):
                pool.dma_start(gidx[:, :], slot_token[bass.ds(p * P, P), :]).then_inc(idx_loaded, 16)
                wait_apart(pool, rounds_ready, idx_loaded, p1 * 16)
                pool.indirect_dma_start(out=rows, out_offset=None, in_=xn2_rows[:, :],
                                        in_offset=bass.IndirectOffsetOnAxis(ap=gidx[:, :], axis=0)).then_inc(rows_gathered, 16)
            pool.sem_inc(y_free, 1)
            gather(0, 1)
            with pool.Fori(0, nr * NPAIR) as p:
                pool.wait_ge(rows_gathered, (p + 1) * 16)
                pool.wait_ge(rows_t_done, p + 1)
                gather(p + 1, p + 2)
                pool.wait_ge(y_out, p * 2 + 3)
                pool.dma_start(slot_out[bass.ds(p * P, P), :].rearrange("(e s) n -> s e n", e=2), ysb[0:CAP]).then_inc(y_stored, 16)
                pool.wait_ge(y_stored, (p + 1) * 16)
                pool.sem_inc(y_free, 1)
            wait_apart(pool, rounds_ready, y_stored, nr * (NPAIR * 16))
            wait_apart(pool, rounds_ready, rows_gathered, nr * (NPAIR * 16) + 16)
            wait_apart(pool, rounds_ready, xgt_ready, nr * NPAIR + 1)
            wait_apart(pool, rounds_ready, groups_done, nr * (NPAIR * 12) + G_MOE)

            def results(table):
                for c, dst in enumerate((y1, y2)):
                    for i, (t, n) in enumerate(TT):
                        pool.indirect_dma_start(out=dst[0:n, i, :], out_offset=None, in_=table,
                                                in_offset=bass.IndirectOffsetOnAxis(ap=slot_i[0:n, c, i:i + 1], axis=0)).then_inc(y_loaded, 16)
            with pool.If(nr > 1):
                results(slot_out[:, :])
            with pool.Else():
                results(slot_out[0:ROUND_ROWS, :])
            pool.wait_ge(fin_out, 3)
            for i, (r, p0, n) in enumerate([(0, NM, P - NM), (P - NM, 0, P), (2 * P - NM, 0, PL)]):
                pool.dma_start(O["y_p"][0, r:r + n, :], xtok[p0:p0 + n, i, :]).then_inc(out_stored, 16)
            pool.dma_start(O["y_s"][0], xtok[PL:NL, 2, :]).then_inc(out_stored, 16)
            pool.wait_ge(cn_stored, 32 * NH)
            pool.wait_ge(out_stored, 16 * 12)


def kernel(**inputs):
    import numpy as np
    import concourse.bacc as bacc
    from concourse import mybir
    from concourse.bass_utils import run_bass_kernel_spmd

    nc = bacc.Bacc("TRN2", target_bir_lowering=False, num_devices=1)
    arrays, A, O = {}, {}, {}
    for name, value in inputs.items():
        a = np.ascontiguousarray(value)
        arrays["in_" + name] = a
        A[name] = nc.dram_tensor("in_" + name, a.shape, mybir.dt.from_np(a.dtype), kind="ExternalInput").ap()
    shapes = {"y_p": inputs["x_prompt"].shape, "y_s": inputs["x_sample"].shape}
    for s, b in (("p", inputs["x_prompt"].shape[0]), ("s", inputs["x_sample"].shape[0])):
        for k, name in (("conv", "state_rglru_conv"), ("h", "state_rglru_h"), ("C", "state_mlstm_C"),
                        ("n", "state_mlstm_n"), ("m", "state_mlstm_m")):
            full = inputs[name].shape
            shapes[s + "_" + k] = (full[0], b) + tuple(full[2:])
    for key, shape in shapes.items():
        O[key] = nc.dram_tensor("out_" + key, tuple(shape), mybir.dt.float32, kind="ExternalOutput").ap()
    build(nc, A, O)
    r = run_bass_kernel_spmd(nc, [arrays], core_ids=[0]).results[0]
    return tuple(r["out_" + key] for key in shapes)
```

```python
def build(nc, A, O):
    import concourse.bass as bass
    from concourse import mybir
    from contextlib import ExitStack

    F32, I32, F32R = mybir.dt.float32, mybir.dt.int32, mybir.dt.float32r
    ACT, ALU, AX = mybir.ActivationFunctionType, mybir.AluOpType, mybir.AxisListType
    P = 128

    NM, DM = A["meta_tokens"].shape
    NP, NS = A["x_prompt"].shape[1], A["x_sample"].shape[1]
    TP = NM + NP
    T = TP + NS
    DR = A["conv_w"].shape[2]
    CW = A["conv_w"].shape[1]
    NB, RB = A["rg_a_w"].shape[1], A["rg_a_w"].shape[2]
    NH, DQK, DV = A["state_mlstm_C"].shape[2:]
    NG, NE = A["w_router_group"].shape[2], A["w_router_expert"].shape[2]
    EG = NE // NG
    DE = A["w_exp_gate"].shape[3]
    EPS = 1e-6
    KD = DM // P
    KR = DR // P
    KE = DE // P
    TT = [(0, P), (P, P), (2 * P, T - 2 * P)]
    NL = TT[2][1]
    PL = TP - 2 * P
    G = 4
    GT = KR // G
    BG = NB // G
    PADDED = T + 2 * (CW - 1)
    CONV = PADDED - (CW - 1)
    S0 = TP + CW - 1
    SEED = 4
    NEG = -1e30
    C_Q = 2 * DR
    C_V = C_Q + 2 * NH * DQK
    C_OG = C_V + NH * DV
    C_GIF = C_OG + NH * DV
    C_MG = C_GIF + 2 * NH
    CAP = P // 2
    NPAIR = NE // 2
    MAXR = -(-T // CAP)
    ROUND_ROWS = NE * CAP
    SLOTS = MAXR * ROUND_ROWS

    w_in = A["w_in"][0].rearrange("(k p) n -> p k n", p=P)
    w_pr = A["w_proj_rnn"][0].rearrange("(k p) n -> p k n", p=P)
    w_pm = A["w_proj_mlstm"][0].rearrange("(k p) n -> p k n", p=P)
    w_out = A["w_out"][0].rearrange("(k p) n -> p k n", p=P)
    w_eg = A["w_exp_gate"][0].rearrange("e (k p) n -> p e k n", p=P)
    w_eu = A["w_exp_up"][0].rearrange("e (k p) n -> p e k n", p=P)
    w_ed = A["w_exp_down"][0].rearrange("e (k p) n -> p e k n", p=P)

    xn2_rows = nc.dram_tensor("xn2_rows", (T, DM), F32)
    slot_token = nc.dram_tensor("slot_token", (SLOTS + P, 1), I32)
    slot_out = nc.dram_tensor("slot_out", (SLOTS, DM), F32)

    ctx = ExitStack()
    with ctx:
        place = {}

        def sb(name, shape, dt=F32):
            place[name] = (nc.sbuf_base + 31) // 32 * 32
            return ctx.enter_context(nc.sbuf_tensor(name, shape, dt))

        def rounded(name, host, at, words):
            return nc.alloc_sbuf_tensor_at(name, [P, words], F32R, offset=place[host] + 4 * at)[:, :]

        def sem(name):
            return ctx.enter_context(nc.semaphore(name))

        def bcast(row):
            return row.partition_broadcast(P)

        UW = KD * 2 * P
        ring = sb("ring", [P, 4, UW])
        XNT = sb("XNT", [P, KD, T])
        OG = sb("OG", [P, KD, T])
        BW = 2 * T + 3 * DV
        HB = sb("HB", [P, NH, BW])
        XG = sb("XG", [P, 2 * KR, PADDED])
        ident = sb("ident", [P, P])
        ones = sb("ones", [P, P])
        before = sb("before", [P, P])
        tri = sb("tri", [P, TP])
        trl = sb("trl", [NL, NL])
        vec = sb("vec", [P, 320])
        CL = sb("CL", [P, KR])
        wgif = sb("wgif", [P, KD, 2 * NH])
        wrt = sb("wrt", [P, KD, NG + NE])
        AB = sb("AB", [P, GT, CONV])
        ST = sb("ST", [P, 2, CW * KR])
        small = sb("small", [P, 24])
        gtok = sb("gtok", [P, 3, 3 * NH])
        hb16 = sb("hb16", [P, 2 * NH])
        nst = sb("nst", [P, 3 * NH])
        gates8 = sb("gates8", [NH, 12])

        XGf = XG[:, :, :].rearrange("p a b -> p (a b)")
        HBf = HB[:, :, :].rearrange("p a b -> p (a b)")
        OGf = OG[:, :, :].rearrange("p a b -> p (a b)")
        HALF = 3 * DM
        xtok = XGf[:, 0:HALF].rearrange("p (a b) -> p a b", a=3)
        xntok = XGf[:, HALF:2 * HALF].rearrange("p (a b) -> p a b", a=3)
        vstage = HBf[:, 0:3 * P].rearrange("p (a b) -> p a b", a=3)
        junk = HBf[:, 512:512 + DM]

        HV0 = 2 * T
        bd = [[HB[:, i, HV0 + m * 3 * P:HV0 + (m + 1) * 3 * P] for i in range(GT)] for m in range(2)]
        RT = [HB[:, GT + j // 2, HV0 + (j % 2) * 3 * P:HV0 + (j % 2) * 3 * P + CONV] for j in range(GT)]
        tmp = HB[:, NH - 1, HV0 + 3 * P:HV0 + 3 * P + CONV]

        at = [0]

        def ml(n):
            at[0] += n
            assert at[0] <= KR * PADDED
            return XGf[:, at[0] - n:at[0]]
        negM, expnm = ml(T), ml(T)
        rows0 = at[0]
        kh, qh, vh = ml(T), ml(T), ml(3 * DV)
        DW = T + TP - P - NS + NL
        dw, hh, sq = ml(DW), ml(2 * T), ml(2 * T)
        rd, es, kp, ks = ml(T), ml(T), ml(3 * DQK), ml(DQK)
        c0, cn = ml(DV), ml(2 * DV)
        FREE_EARLY = (at[0] - 3 * DV) // T
        selM, selE = ml(T), ml(T)
        at[0] = rows0
        li, lf, bc, gg, wp, ws, t0, t1 = (ml(T)[0:NH] for _ in range(8))
        small2 = sb("small2", [P, NS])
        kc = sb("kc", [P, NE + EG])
        tokid = sb("tokid", [P, 3], I32)
        nrounds = sb("nrounds", [P, 1], I32)
        slot_i = sb("slot_i", [P, 2, 3], I32)
        gidx = sb("gidx", [P, 1], I32)
        RTW = sb("RTW", [P, 6])

        bank = [ctx.enter_context(nc.psum_tensor(f"bank{i}", [P, 512], F32)) for i in range(8)]

        V_N1, V_N2, V_MN, V_CB = 0, KD, 2 * KD, 3 * KD
        V_AB, V_XB, V_LM = V_CB + KR, V_CB + 2 * KR, V_CB + 3 * KR
        V_CW, V_H0, V_CS = P, P + CW * KR, 2 * P

        SC = [(P, 0, TP, 0), (P, TP, TP - P, P), (NL, TP + TP - P, NL, 2 * P)]

        slot_full = [sem(f"slot_full{b}") for b in range(4)]
        groups_done, dve_evac, act_evac = sem("groups_done"), sem("dve_evac"), sem("act_evac")
        dve_steps, act_steps = sem("dve_steps"), sem("act_steps")

        n0b = sq[:, 0:P]
        diag8 = sb("diag8", [NH, 2 * NH])[:, :]
        zeros_i = sb("zeros_i", [P, (SLOTS + P) // P], I32)
        junk2 = HBf[:, 8000:8000 + DM]
        xn2t = HBf[:, KD // 4 * BW:KD // 4 * BW + KD * T].rearrange("p (k t) -> p k t", k=KD)
        rows = HBf[:, 0:DM]
        xs = rounded("xs", "HB", DM, 2 * DM).rearrange("p (k e c) -> p k e c", k=KD, e=2)
        ysb = HBf[:, 3 * DM:5 * DM].rearrange("p (e n) -> p e n", e=2)

        def half(slot, ru, c):
            if ru % 6 < 4:
                return slot[:, c * HW:(c + 1) * HW].rearrange("p (k n) -> p k n", k=KE)
            return slot.rearrange("p (k n) -> p k n", k=KE)[:, :, c * DE:(c + 1) * DE]

        HW = UW // 2
        w_raw = [ring[:, b, :] for b in range(4)]
        w_low = [rounded(f"w_low{b}", "ring", b * UW, UW) for b in range(4)]
        XKf = XGf[:, HALF:2 * HALF]
        w_high = [rounded(f"w_high{c}", "XNT" if c < 2 else "XG", (0 if c < 2 else HALF) + c % 2 * HW, HW)
                  .rearrange("p (k n) -> p k n", k=KE) for c in range(4)]
        HC = KE * CAP
        gu = XKf[:, UW:UW + 2 * DE].rearrange("p (a n) -> p a n", a=2)
        sg = XKf[:, UW + 2 * DE:UW + 2 * DE + HC]
        hf = XKf[:, UW + 2 * DE + HC:UW + 2 * DE + 2 * HC]
        hs_high = rounded("hs_high", "XG", HALF + UW + 2 * DE + 2 * HC, HC)
        hs_low = rounded("hs_low", "XG", HALF + UW + 2 * DE + 3 * HC, HC)
        add2 = tri[:, 0:CAP]
        x_high = rounded("x_high", "XNT", 0, KD * T).rearrange("p (k t) -> p k t", k=KD)
        x_low = rounded("x_low", "OG", 0, KD * T).rearrange("p (k t) -> p k t", k=KD)
        TW = KD * P
        t_high = [rounded(f"t_high{c}", "HB", 5 * BW + c * TW, TW).rearrange("p (k n) -> p k n", k=KD) for c in range(2)]

        hb_rounded = rounded("hb_rounded", "HB", 0, NH * BW).rearrange("p (h n) -> p h n", h=NH)
        p_high = [rounded(f"p_high{c}", "XG", KR * PADDED + c * TW, TW).rearrange("p (k n) -> p k n", k=KD) for c in range(2)]

        xg_rounded = rounded("xg_rounded", "XG", 0, 2 * KR * PADDED).rearrange("p (k t) -> p k t", k=2 * KR)
        yr_high = rounded("yr_high", "XG", 0, KR * T).rearrange("p (k t) -> p k t", k=KR)
        KQ = KR // 4
        q_high = [rounded(f"q_high{c}", ("ring", "AB")[c // 2], (3 * UW + KR * P if c < 2 else 0) + c % 2 * KQ * P, KQ * P)
                  .rearrange("p (k n) -> p k n", k=KQ) for c in range(4)]

        def quarter(slot, c):
            return slot[:, c * KQ * P:(c + 1) * KQ * P].rearrange("p (k n) -> p k n", k=KQ)

        def tile_of(slot, f):
            return slot.rearrange("p (k n) -> p k n", k=KD)[:, :, f * P:(f + 1) * P]

        y1 = xntok
        y2 = HBf[:, 0:HALF].rearrange("p (a b) -> p a b", a=3)
        nb2, nbf = OGf[:, 0:DM], OGf[:, DM:2 * DM]
        rt_at = [2 * DM]

        def rt(n, a=3):
            rt_at[0] += a * n
            assert rt_at[0] <= KD * T
            return OGf[:, rt_at[0] - a * n:rt_at[0]].rearrange("p (a n) -> p a n", a=a)
        brt = rt(NG + NE, 1)[:, 0, :]
        gl, el = rt(NG), rt(NE)
        gmx, gkey, goh = rt(1), rt(NG), rt(NG)
        prod = rt(NE)
        ein, ekey, o1, o2, e2 = rt(EG), rt(EG), rt(EG), rt(EG), rt(EG)
        v1, v2, gw, ex, kmx = rt(1), rt(1), rt(1), rt(1), rt(1)
        E1, E2, picked = rt(NE), rt(NE), rt(NE)
        rk, sl, slt = rt(NE), rt(NE), rt(NE)
        w1, w2, slf = rt(1), rt(1), rt(2)
        cmx = rt(2, 1)[:, 0, :]

        PIECES = []
        for b_ in range(BG):
            r_ = RB * b_
            while r_ < RB * (b_ + 1):
                n_ = min(RB * (b_ + 1), (r_ // P + 1) * P) - r_
                PIECES.append((b_, r_ - RB * b_, n_, r_ // P, r_ % P))
                r_ += n_
        TOUCH = {(i, j) for (b_, _, _, i, _) in PIECES for j in range(GT)
                 if j * P < RB * (b_ + 1) and (j + 1) * P > RB * b_}
        BDP = len(PIECES)
        GATE_SEED = GT + 1
        VA_ROWS, VB_ROWS, VC_ROWS = 3 * KD + 4 * KR, CW * KR + KR, (CW - 1) * KR
        NVEC, NPAR = 10, 6
        G_QK = 2 * KR
        G_V = G_QK + 8 * G
        G_MG = G_V + 3 * NH
        G_PR = G_MG + 2 * KD
        G_PM = G_PR + KD
        G_OUT = G_PM + KD
        G_MOE = G_OUT + KD
        TURNS = 2 * KR // 8 + G + 2 + 4 + KD // 4 + 2 * (KD // 8)
        LOADS_MOE = [TURNS] * 4
        bd_loaded = [sem("bd_loaded_a"), sem("bd_loaded_x")]
        rounds_ready = sem("rounds_ready")
        gate_mm = sem("gate_mm")
        consts_ready = sem("consts_ready")
        vec_loaded = sem("vec_loaded")
        vec_transposed = sem("vec_transposed")
        xn_ready = sem("xn_ready")
        xnt_ready = sem("xnt_ready")
        x_transposed = sem("x_transposed")
        conv_done = sem("conv_done")
        gate_evac = sem("gate_evac")
        par_loaded = sem("par_loaded")
        gif_done = sem("gif_done")
        rows_t = sem("rows_t")
        gt_mm = sem("gt_mm")
        gt_ready = sem("gt_ready")
        staged_a = sem("staged_a")
        staged_d = sem("staged_d")
        pe_scores = sem("pe_scores")
        sw_ready = sem("sw_ready")
        es_ready = sem("es_ready")
        c0_loaded = sem("c0_loaded")
        pe_num = sem("pe_num")
        pe_kt = sem("pe_kt")
        h_ready = sem("h_ready")
        sq_h = sem("sq_h")
        pe_ss = sem("pe_ss")
        kp_ready = sem("kp_ready")
        pe_cn = sem("pe_cn")
        group_done = sem("group_done")
        head_done = sem("head_done")
        st_t = sem("st_t")
        x2_ready = sem("x2_ready")
        x2_t = sem("x2_t")
        xn2_ready = sem("xn2_ready")
        xn2t_ready = sem("xn2t_ready")
        xn2_t = sem("xn2_t")
        st_ready = sem("st_ready")
        logits = sem("logits")
        chosen = sem("chosen")
        rank_mm = sem("rank_mm")
        rows_gathered = sem("rows_gathered")
        rows_t_done = sem("rows_t_done")
        xgt_ready = sem("xgt_ready")
        h_act = sem("h_act")
        xn_made = sem("xn_made")
        xn_split = sem("xn_split")
        t_split = sem("t_split")
        t_rest = sem("t_rest")
        xnt_whole = sem("xnt_whole")
        yr_split = sem("yr_split")
        yr_rest = sem("yr_rest")
        q_split = sem("q_split")
        q_rest = sem("q_rest")
        q_used = sem("q_used")
        ym_split = sem("ym_split")
        ym_rest = sem("ym_rest")
        mix_split = sem("mix_split")
        mix_rest = sem("mix_rest")
        w_split = sem("w_split")
        add2_ready = sem("add2_ready")
        w_rest = sem("w_rest")
        halves_used = sem("halves_used")
        gu_copied = sem("gu_copied")
        gu_summed = sem("gu_summed")
        xs_high = sem("xs_high")
        h_steps = sem("h_steps")
        y_out = sem("y_out")
        y_free = sem("y_free")
        x_loaded = sem("x_loaded")
        ss_init = sem("ss_init")
        ss_done = sem("ss_done")
        var_ready = sem("var_ready")
        std_ready = sem("std_ready")
        lam_abs = sem("lam_abs")
        lam_exp = sem("lam_exp")
        gelu_done = sem("gelu_done")
        gated = sem("gated")
        a_ready = sem("a_ready")
        sq_ready = sem("sq_ready")
        sqrt_done = sem("sqrt_done")
        z_abs = sem("z_abs")
        z_exp = sem("z_exp")
        mrow_ready = sem("mrow_ready")
        row_exp = sem("row_exp")
        og_ready = sem("og_ready")
        d_ready = sem("d_ready")
        wi_ready = sem("wi_ready")
        w_ready = sem("w_ready")
        vr_ready = sem("vr_ready")
        sr_ready = sem("sr_ready")
        mg_ready = sem("mg_ready")
        cn_stored = sem("cn_stored")
        nb_loaded = sem("nb_loaded")
        ss2_done = sem("ss2_done")
        var2 = sem("var2")
        std2 = sem("std2")
        cols_e = sem("cols_e")
        exps_e = sem("exps_e")
        silu_done = sem("silu_done")
        fin_ss = sem("fin_ss")
        fin_sq = sem("fin_sq")
        fin_var = sem("fin_var")
        fin_std = sem("fin_std")
        cn_ready = sem("cn_ready")
        vec_ready = sem("vec_ready")
        states_saved = sem("states_saved")
        xr_loaded = sem("xr_loaded")
        y_loaded = [sem(f"y_loaded{i}") for i in range(3)]
        fin_out = sem("fin_out")
        zeroed = sem("zeroed")
        out_stored = sem("out_stored")
        xn2_stored = sem("xn2_stored")
        perm_written = sem("perm_written")
        rest_zeroed = sem("rest_zeroed")
        idx_loaded = sem("idx_loaded")
        y_stored = sem("y_stored")
        pool_steps = sem("pool_steps")

        def wait_apart(eng, reached, counter, value):
            value = eng.to_reg(value)
            eng.wait_ge(reached, 1)
            eng.wait_ge(counter, value)

        class Steps:

            def __init__(self, eng, counter):
                self.eng, self.counter, self.base, self.n = eng, counter, 0, 0

            def step(self, ins, beside=None):
                ins.then_inc(self.counter, 1)
                self.n += 1
                if beside is None:
                    self.eng.wait_ge(self.counter, self.base + self.n)
                else:
                    wait_apart(self.eng, beside, self.counter, self.base + self.n)

            def enter(self, i, per):
                self.start, self.per = self.base + self.n, per
                self.base, self.n = self.start + i * per, 0

            def leave(self, count):
                assert self.n == self.per, (self.n, self.per)
                self.base, self.n = self.start + count * self.per, 0

        block = ctx.enter_context(nc.Block())

        @block.sync
        def _(sp):
            freed = [None] * 4

            def stream(iters, groups, start, unit):
                def load(i, b):
                    dst, src = unit(i, b)
                    sp.dma_start(dst, src).then_inc(slot_full[b], 16)
                for b in range(4):
                    if freed[b] is not None:
                        sp.wait_ge(groups_done, freed[b])
                    load(0, b)
                if iters > 1:
                    with sp.Fori(0, iters - 1) as i:
                        for b in range(4):
                            sp.wait_ge(groups_done, i * (4 * groups) + start + (b + 1) * groups)
                            load(i + 1, b)
                for b in range(4):
                    freed[b] = start + (iters - 1) * 4 * groups + (b + 1) * groups
                return start + iters * 4 * groups

            def full(b):
                return ring[:, b, :].rearrange("p (k n) -> p k n", k=KD)

            def wide(w, first):
                return lambda i, b: (full(b), w[:, :, bass.ds(i * (8 * P) + (first + b * 2 * P), 2 * P)])

            sp.wait_ge(x_loaded, 16 * 5)
            g = stream(2 * KR // 8, 2, 0, wide(w_in, 0))
            g = stream(2, 2, g, wide(w_in, C_Q))
            g = stream(2, 2, g, wide(w_in, C_OG))
            g = stream(2, 3, g, wide(w_in, C_V))
            g = stream(4, 2, g, wide(w_in, C_MG))
            g = stream(KD // 4, 1, g, lambda i, b: (
                ring[:, b, 0:KR * P].rearrange("p (k n) -> p k n", k=KR),
                w_pr[:, :, bass.ds(i * (4 * P) + b * P, P)]))
            g = stream(KD // 8, 2, g, wide(w_pm, 0))
            g = stream(KD // 8, 2, g, wide(w_out, 0))
            assert g == G_MOE

            def expert_unit(e, k):
                if k < 4:
                    w, h = (w_eg if k < 2 else w_eu), KD // 2
                    return w[:, e, (k % 2) * h:(k % 2 + 1) * h, :].rearrange("p e k n -> p (e k) n")
                hw = DM // 2
                return w_ed[:, e, :, (k - 4) * hw:(k - 3) * hw].rearrange("p e k n -> p (e k) n")

            def unit_view(b, k):
                return ring[:, b, :].rearrange("p (k n) -> p k n", k=(KD // 2 if k < 4 else KE))

            for b in range(4):
                sp.wait_ge(groups_done, freed[b])
                sp.dma_start(unit_view(b, b), expert_unit(slice(0, 1), b)).then_inc(slot_full[b], 16)
            sp.wait_ge(rounds_ready, 1)
            n = sp.value_load(nrounds[0:1, 0:1], min_val=1, max_val=MAXR)


            def pair(q, turn):
                for u in range(4, 12):
                    sp.wait_ge(groups_done, turn * 12 + (G_MOE + u - 3))
                    sp.dma_start(unit_view(u % 4, u % 6), expert_unit(bass.ds(q * 2 + u // 6, 1), u % 6)
                                 ).then_inc(slot_full[u % 4], 16)

            with sp.Fori(0, n * NPAIR - 1) as t:
                pair(t % NPAIR, t)
                for b in range(4):
                    sp.wait_ge(groups_done, t * 12 + (G_MOE + 8 + b + 1))
                    sp.dma_start(unit_view(b, b), expert_unit(bass.ds(((t + 1) % NPAIR) * 2, 1), b)).then_inc(slot_full[b], 16)
            pair(NPAIR - 1, n * NPAIR - 1)
            sp.wait_ge(groups_done, n * (NPAIR * 12) + (G_MOE - 12 + 8 + 1))
            sp.dma_start(unit_view(0, 0), expert_unit(slice(0, 1), 0)).then_inc(slot_full[0], 16)
            for b in range(4):
                wait_apart(sp, rounds_ready, slot_full[b], n * (NPAIR * 3 * 16) + (LOADS_MOE[b] + (1 if b == 0 else 0)) * 16)

        @block.tensor
        def _(pe):
            for counter in (pe_scores, pe_kt, pe_num, pe_ss, pe_cn):
                pe.sem_inc(counter, 1)
            pe.sem_inc(gate_mm, GATE_SEED)

            pe.wait_ge(consts_ready, 1)
            pe.wait_ge(vec_loaded, 16 * NVEC)
            for c, n in ((0, P), (1, VB_ROWS), (2, VC_ROWS)):
                last = pe.transpose(bank[4][:, c * P:c * P + n], vstage[0:n, c, :], ident[0:n, 0:n])
            last.then_inc(vec_transposed, 1)
            pe.wait_ge(xn_ready, 3)
            for k in range(KD):
                if k >= 4:
                    pe.wait_ge(xnt_ready, k - 3)
                for i, (t, n) in enumerate(TT):
                    last = pe.transpose(bank[k % 4][:, t:t + n], xntok[0:n, i, k * P:(k + 1) * P], ident[0:n, 0:n])
                last.then_inc(x_transposed, 1)
            pe.wait_ge(xnt_ready, KD)

            def dense(i, turn, jj, evac, seen, rhs):
                b = jj // 2
                if jj % 2 == 0:
                    pe.wait_ge(slot_full[b], (i + (turn + 1)) * 16)
                pe.wait_ge(evac, i * 8 + (seen + jj + SEED - 3))
                w = tile_of(ring[:, b, :], jj % 2)
                for k in range(KD):
                    last = pe.matmul(bank[jj % 4][:, 0:T], w[:, k, :], rhs(k), start=(k == 0), stop=(k == KD - 1))
                last.then_inc(groups_done, 1)

            def xnt(k):
                return XNT[:, k, :]

            turn = 0
            n = 2 * KR // 8

            def split_product(jj, tiles, evacuated, w_high_, rhs_high, rhs_low):
                pe.wait_ge(t_rest, tiles)
                pe.wait_ge(dve_evac, evacuated)
                high, low = w_high_[jj % 2], tile_of(w_low[jj // 2], jj % 2)
                dst = bank[jj % 4][:, 0:T]
                for k in range(KD):
                    pe.matmul(dst, high[:, k, :], rhs_high(k), start=(k == 0), stop=False)
                    pe.matmul(dst, high[:, k, :], rhs_low(k), start=False, stop=False)
                    last = pe.matmul(dst, low[:, k, :], rhs_high(k), start=False, stop=(k == KD - 1))
                last.then_inc(groups_done, 1)

            with pe.Fori(0, n) as i:
                for jj in range(8):
                    split_product(jj, i * 8 + (jj + 1), i * 8 + (jj + SEED - 3), t_high,
                                  lambda k: x_high[:, k, :], lambda k: x_low[:, k, :])
            turn += n
            dve_seen, act_seen = 2 * KR, 0
            pe.wait_ge(dve_evac, SEED + dve_seen)
            pe.wait_ge(xnt_whole, 1)

            with pe.Fori(0, G) as g:
                for m in range(2):
                    for jj in range(4 * m, 4 * m + 4):
                        dense(g, turn, jj, act_evac, act_seen, xnt)
                    pe.wait_ge(bd_loaded[m], (g + 1) * (16 * BDP))
                    pe.wait_ge(conv_done, (g + 1) * GT)
                    for j in range(GT):
                        pe.wait_ge(gate_evac, g * (2 * GT) + (SEED + m * GT + (1 if j == 4 else 0)))
                        src = [i for i in (j - 1, j, j + 1) if (i, j) in TOUCH]
                        for i in src:
                            last = pe.matmul(bank[4 + j % 4][:, 0:CONV], bd[m][i][:, (j - i + 1) * P:(j - i + 2) * P],
                                             XG[:, bass.ds(g * GT + i, 1), 0:CONV].rearrange("p a t -> p (a t)"),
                                             start=(i == src[0]), stop=(i == src[-1]))
                        last.then_inc(gate_mm, 1)
            turn += G
            act_seen += 8 * G
            pe.wait_ge(act_evac, SEED + act_seen)

            pe.wait_ge(par_loaded, 16 * NPAR)
            pe.wait_ge(gate_evac, SEED + 2 * KR)
            for c in range(2):
                for k in range(KD):
                    last = pe.matmul(bank[4 + c][0:NH, 0:T], wgif[:, k, c * NH:(c + 1) * NH], XNT[:, k, :],
                                     start=(k == 0), stop=(k == KD - 1))
                last.then_inc(gif_done, 1)

            with pe.Fori(0, 2) as i:
                for b in range(4):
                    pe.wait_ge(slot_full[b], (i + (turn + 1)) * 16)
                    for c, (t, n) in enumerate(TT):
                        jj = b * 3 + c
                        pe.wait_ge(dve_evac, i * 12 + (dve_seen + jj + SEED - 3))
                        for k in range(KD):
                            last = pe.matmul(bank[jj % 4][0:n, 0:2 * P], XNT[:, k, t:t + n],
                                             ring[:, b, k * 2 * P:(k + 1) * 2 * P], start=(k == 0), stop=(k == KD - 1))
                        last.then_inc(groups_done, 1)
            turn += 2
            dve_seen += 24
            pe.wait_ge(dve_evac, SEED + dve_seen)

            pe.wait_ge(rows_t, 1)
            for c, row in enumerate((gg, wp, ws)):
                for i, (t, n) in enumerate(TT):
                    pe.transpose(bank[6][0:n, (i * 3 + c) * NH:(i * 3 + c + 1) * NH], row[:, t:t + n], ident[0:NH, 0:NH])
            pe.matmul(bank[7][:, 0:2 * NH], ones[0:NH, :], diag8, start=True, stop=True).then_inc(gt_mm, 1)
            pe.wait_ge(gt_ready, 1)

            with pe.Fori(0, NH // 2) as hp:
                for e in range(2):
                    h1 = hp * 2 + (e + 1)
                    dense(hp, turn, 4 * e, act_evac, act_seen, xnt)
                    pe.wait_ge(staged_a, h1)
                    pe.wait_ge(staged_d, h1)
                    for m, c, n, t in SC:
                        pe.matmul(bank[4][0:m, c:c + n], kh[:, t:t + m], qh[:, t:t + n], start=True, stop=True)
                    pe.matmul(bank[5][:, 0:T], ones[0:NH, :], selM[0:NH], start=True, stop=True)
                    pe.matmul(bank[6][:, 0:T], ones[0:NH, :], selE[0:NH], start=True, stop=True).then_inc(pe_scores, 1)
                    dense(hp, turn, 4 * e + 1, act_evac, act_seen, xnt)
                    pe.wait_ge(sw_ready, h1)
                    pe.wait_ge(es_ready, h1)
                    pe.wait_ge(c0_loaded, h1 * 16)
                    for b, lt in ((5, None), (6, 0), (7, 1)):
                        def left(i, n):
                            return ones[0:n, :] if lt is None else vh[0:n, i * DV + lt * P:i * DV + (lt + 1) * P]
                        pe.matmul(bank[b][:, 0:TP], left(0, P), dw[:, 0:TP], start=True, stop=False)
                        pe.matmul(bank[b][:, P:TP], left(1, P), dw[:, TP:TP + TP - P], start=False, stop=False)
                        c = SC[2][1]
                        pe.matmul(bank[b][:, 2 * P:TP], left(2, NL), dw[0:NL, c:c + PL], start=False, stop=False)
                        pe.matmul(bank[b][:, TP:T], left(2, NL), dw[0:NL, c + PL:c + NL], start=False, stop=False)
                        l0 = n0b if lt is None else c0[:, lt * P:(lt + 1) * P]
                        last = pe.matmul(bank[b][:, TP:T], l0, small2[:, :], start=False, stop=True)
                    last.then_inc(pe_num, 1)
                    dense(hp, turn, 4 * e + 2, act_evac, act_seen, xnt)
                    for i, (t, n) in enumerate(TT):
                        last = pe.transpose(bank[4][0:n, i * P:(i + 1) * P], kh[:, t:t + n], ident[:, :])
                    last.then_inc(pe_kt, 1)
                    pe.wait_ge(h_ready, h1)
                    pe.wait_ge(sq_h, h1)
                    for c in range(2):
                        last = pe.matmul(bank[5][:, 0:T], ones[:, :], sq[:, c * T:(c + 1) * T], start=(c == 0), stop=(c == 1))
                    last.then_inc(pe_ss, 1)
                    dense(hp, turn, 4 * e + 3, act_evac, act_seen, xnt)
                    pe.wait_ge(kp_ready, h1)
                    for c, rhs in ((0, None), (1, ones)):
                        dst = bank[6][:, 0:DV] if c == 0 else bank[7][:, 0:1]
                        for i, (t, n) in enumerate(TT):
                            r_ = vh[0:n, i * DV:(i + 1) * DV] if c == 0 else ones[0:n, 0:1]
                            pe.matmul(dst, kp[0:n, i * DQK:(i + 1) * DQK], r_, start=(i == 0), stop=(i == 2))
                        dst = bank[6][:, DV:2 * DV] if c == 0 else bank[7][:, 1:2]
                        r_ = vh[0:NL, 2 * DV:3 * DV] if c == 0 else ones[0:NL, 0:1]
                        last = pe.matmul(dst, ks[0:NL, :], r_, start=True, stop=True)
                    last.then_inc(pe_cn, 1)
            turn += 4
            act_seen += 2 * KD
            pe.wait_ge(act_evac, SEED + act_seen)

            pe.wait_ge(group_done, G + 1)
            pe.wait_ge(yr_rest, KQ)
            with pe.Fori(0, KD // 4) as i:
                for jj in range(4):
                    pe.wait_ge(dve_evac, i * 4 + (dve_seen + jj + SEED - 3))
                    for c in range(4):
                        pe.wait_ge(q_rest, i * 16 + (4 * jj + c + 1))
                        high, low = q_high[c], quarter(w_low[jj], c)
                        for k in range(KQ):
                            kk = c * KQ + k
                            yh, yl = yr_high[:, kk, :], xg_rounded[:, KR + kk, 0:T]
                            pe.matmul(bank[jj][:, 0:T], high[:, k, :], yh, start=(kk == 0), stop=False)
                            pe.matmul(bank[jj][:, 0:T], high[:, k, :], yl, start=False, stop=False)
                            last = pe.matmul(bank[jj][:, 0:T], low[:, k, :], yh, start=False, stop=(kk == KR - 1))
                        last.then_inc(q_used if c < 3 else groups_done, 1)
            turn += KD // 4
            dve_seen += KD
            pe.wait_ge(head_done, NH)
            pe.wait_ge(ym_rest, KD)
            with pe.Fori(0, KD // 8) as i:
                for jj in range(8):
                    split_product(jj, i * 8 + (2 * KR + jj + 1), i * 8 + (dve_seen + jj + SEED - 3), p_high,
                                  lambda k: x_high[:, k, :], lambda k: x_low[:, k, :])
            turn += KD // 8
            dve_seen += KD
            pe.wait_ge(mix_rest, KD)
            with pe.Fori(0, KD // 8) as i:
                for jj in range(8):
                    split_product(jj, i * 8 + (2 * KR + KD + jj + 1), i * 8 + (dve_seen + jj + SEED - 3), p_high,
                                  lambda k: hb_rounded[:, NH // 2 + k // 4, (k % 4) * T:(k % 4 + 1) * T],
                                  lambda k: hb_rounded[:, k // 4, (k % 4) * T:(k % 4 + 1) * T])
            turn += KD // 8
            dve_seen += KD
            pe.wait_ge(dve_evac, SEED + dve_seen)

            for c in range(2):
                last = pe.transpose(bank[4 + c][0:CW * KR, 0:P], ST[:, c, :], ident[:, :])
            last.then_inc(st_t, 1)
            for i, (t, n) in enumerate(TT):
                for q in range(KD // 4):
                    u = i * (KD // 4) + q
                    if u >= 4:
                        pe.wait_ge(x2_ready, u - 3)
                    for k in range(4 * q, 4 * q + 4):
                        last = pe.transpose(bank[u % 4][0:n, (k % 4) * P:(k % 4 + 1) * P], XNT[:, k, t:t + n], ident[:, :])
                    last.then_inc(x2_t, 1)
            pe.wait_ge(x2_ready, 3 * KD // 4)
            pe.wait_ge(xn2_ready, 3)
            for k in range(KD):
                if k >= 4:
                    pe.wait_ge(xn2t_ready, k - 3)
                for i, (t, n) in enumerate(TT):
                    last = pe.transpose(bank[k % 4][:, t:t + n], xntok[0:n, i, k * P:(k + 1) * P], ident[0:n, 0:n])
                last.then_inc(xn2_t, 1)
            pe.wait_ge(xn2t_ready, KD)
            pe.wait_ge(st_ready, 1)
            R = NG + NE
            for i, (t, n) in enumerate(TT):
                for k in range(KD):
                    last = pe.matmul(bank[4][0:n, i * R:(i + 1) * R], xn2t[:, k, t:t + n], wrt[:, k, :],
                                     start=(k == 0), stop=(k == KD - 1))
            last.then_inc(logits, 1)
            pe.wait_ge(chosen, 1)
            for i, (t, n) in enumerate(TT):
                for j in range(i + 1):
                    m = TT[j][1]
                    pe.matmul(bank[5][0:n, i * NE:(i + 1) * NE], (before if j == i else ones)[0:m, 0:n],
                              picked[0:m, j, :], start=(j == 0), stop=(j == i))
            for j, (_, m) in enumerate(TT):
                last = pe.matmul(bank[6][:, 0:NE], ones[0:m, :], picked[0:m, j, :], start=(j == 0), stop=(j == 2))
            last.then_inc(rank_mm, 1)

            pe.wait_ge(add2_ready, 1)
            pe.sem_inc(halves_used, 2)
            pe.wait_ge(rounds_ready, 1)
            nr = pe.value_load(nrounds[0:1, 0:1], min_val=1, max_val=MAXR)

            def gather_transpose(p1):
                pe.wait_ge(rows_gathered, p1 * 16)
                for b in range(4):
                    for c in range(4):
                        k = 4 * b + c
                        last = pe.transpose(bank[b][:, c * P:(c + 1) * P], rows[:, k * P:(k + 1) * P], ident[:, :])
                last.then_inc(rows_t_done, 1)

            gather_transpose(1)
            with pe.Fori(0, nr * NPAIR) as p:
                for e in range(2):
                    if e == 0:
                        pe.wait_ge(xgt_ready, p + 1)
                    for u in range(4):
                        ru, c = 6 * e + u, u // 2
                        if u % 2 == 0:
                            pe.wait_ge(gu_copied, p * 4 + (2 * e + c + 1))
                        for f in range(2):
                            pe.wait_ge(w_rest, p * 24 + (2 * ru + f + 1))
                            high, low = w_high[(2 * ru + f) % 4], half(w_low[ru % 4], ru, f)
                            for k in range(KE):
                                kk = ((u % 2) * 2 + f) * KE + k
                                lhs = xs[:, kk, e, :]
                                pe.matmul(bank[4 + c][:, 0:DE], lhs, high[:, k, :], start=(kk == 0), stop=False)
                                last = pe.matmul(bank[4 + c][:, 0:DE], lhs, low[:, k, :], start=False, stop=(kk == KD - 1))
                            if f == 0:
                                last.then_inc(halves_used, 1)
                        last.then_inc(groups_done, 1)
                    if e == 1:
                        pe.wait_ge(y_out, p * 2 + 2)
                        gather_transpose(p + 2)
                    pe.wait_ge(h_act, p * 2 + (e + 1))
                    for c in range(2):
                        pe.wait_ge(gu_copied, p * 4 + (2 * e + c + 3))
                        for j in range(KE):
                            last = pe.matmul(bank[6][:, (c * KE + j) * CAP:(c * KE + j + 1) * CAP],
                                             gu[:, c, j * P:(j + 1) * P], add2[:, :], start=True, stop=True)
                    last.then_inc(gu_summed, 1)
                    pe.wait_ge(h_act, p * 2 + (e + 2))
                    if e == 0:
                        pe.wait_ge(y_out, p * 2 + 1)
                    else:
                        pe.wait_ge(xgt_ready, p + 2)
                    for u in range(2):
                        ru = 6 * e + 4 + u
                        for c in range(2):
                            pe.wait_ge(w_rest, p * 24 + (2 * ru + c + 1))
                            high, low = w_high[(2 * ru + c) % 4], half(w_low[ru % 4], ru, c)
                            dst = bank[2 * u + c][0:CAP, 0:DE]
                            for k in range(KE):
                                hh, hl = hs_high[:, k * CAP:(k + 1) * CAP], hs_low[:, k * CAP:(k + 1) * CAP]
                                pe.matmul(dst, hh, high[:, k, :], start=(k == 0), stop=False)
                                pe.matmul(dst, hl, high[:, k, :], start=False, stop=False)
                                last = pe.matmul(dst, hh, low[:, k, :], start=False, stop=(k == KE - 1))
                            if c == 0:
                                last.then_inc(halves_used, 1)
                        last.then_inc(groups_done, 1)

        @block.scalar
        def _(act):
            own = Steps(act, act_steps)

            def load_x(done):
                split = [(0, NM, P - NM), (P - NM, 0, P), (2 * P - NM, 0, PL)]
                act.dma_start(xtok[0:NM, 0, :], A["meta_tokens"]).then_inc(done, 16)
                for i, (r, p0, n) in enumerate(split):
                    act.dma_start(xtok[p0:p0 + n, i, :], A["x_prompt"][0, r:r + n, :]).then_inc(done, 16)
                act.dma_start(xtok[PL:NL, 2, :], A["x_sample"][0]).then_inc(done, 16)

            load_x(x_loaded)

            def rows_of(name, k):
                return A[name].rearrange("a (k f) -> (a k) f", k=k)
            r = 0
            for name, k in (("norm1_w", KD), ("norm2_w", KD), ("mlstm_norm_w", KD), ("conv_b", KR),
                            ("rg_a_b", KR), ("rg_x_b", KR), ("rg_lambda", KR)):
                act.dma_start(vstage[r:r + k, 0, :], rows_of(name, k)).then_inc(vec_loaded, 16)
                r += k
            act.dma_start(vstage[0:CW * KR, 1, :], A["conv_w"][0].rearrange("w (k f) -> (w k) f", k=KR)).then_inc(vec_loaded, 16)
            act.dma_start(vstage[CW * KR:VB_ROWS, 1, :], A["state_rglru_h"][0].rearrange("a (k f) -> (a k) f", k=KR)).then_inc(vec_loaded, 16)
            act.dma_start(vstage[0:VC_ROWS, 2, :], A["state_rglru_conv"][0, 0].rearrange("w (k f) -> (w k) f", k=KR)).then_inc(vec_loaded, 16)
            act.dma_start(wgif[:, :, :], w_in[:, :, C_GIF:C_GIF + 2 * NH]).then_inc(par_loaded, 16)
            act.dma_start(wrt[:, :, 0:NG], A["w_router_group"][0].rearrange("(k p) n -> p k n", p=P)).then_inc(par_loaded, 16)
            act.dma_start(wrt[:, :, NG:NG + NE], A["w_router_expert"][0].rearrange("(k p) n -> p k n", p=P)).then_inc(par_loaded, 16)
            act.dma_start(gates8[:, 2:4], A["b_gates"][0].rearrange("(c h) -> h c", h=NH), allow_slow_non_contiguous=True).then_inc(par_loaded, 16)
            act.dma_start(gates8[:, 0:1], A["state_mlstm_m"][0].rearrange("a h -> h a"), allow_slow_non_contiguous=True).then_inc(par_loaded, 16)
            act.dma_start(nst[:, 2 * NH:3 * NH], A["state_mlstm_n"][0, 0].rearrange("h k -> k h"), allow_slow_non_contiguous=True).then_inc(par_loaded, 16)

            act.wait_ge(x_loaded, 16 * 5)
            act.wait_ge(ss_init, 1)
            for i, (t, n) in enumerate(TT):
                act.activation(junk[0:n], xtok[0:n, i, :], ACT.Square, accum_out=small[0:n, i:i + 1]).then_inc(ss_done, 1)
                act.wait_ge(ss_done, i + 1)
            act.wait_ge(var_ready, 1)
            act.activation(small[:, 3:6], small[:, 3:6], ACT.Sqrt).then_inc(std_ready, 1)
            act.wait_ge(lam_abs, 1)
            act.activation(AB[:, 0, 0:KR], AB[:, 0, 0:KR], ACT.Exp, scale=-1.0).then_inc(lam_exp, 1)

            def split_tile(i, jj, first):
                if jj % 2 == 0:
                    act.wait_ge(slot_full[jj // 2], (i + 1) * 16)
                if not (first and jj < 2):
                    act.wait_ge(groups_done, i * 8 + (jj - 1))
                act.activation(t_high[jj % 2], tile_of(w_raw[jj // 2], jj % 2), ACT.Copy).then_inc(t_split, 1)

            split_tile(0, 0, True)
            split_tile(0, 1, True)
            for k in range(KD):
                act.wait_ge(xn_made, k + 1)
                act.activation(x_high[:, k, :], OG[:, k, :], ACT.Copy).then_inc(xn_split, 1)
            for jj in range(2, 8):
                split_tile(0, jj, True)
            with act.Fori(0, 2 * KR // 8 - 1) as i:
                for jj in range(8):
                    split_tile(i + 1, jj, False)

            act.sem_inc(act_evac, SEED)
            act.sem_inc(gate_evac, SEED)
            act.wait_ge(dve_evac, SEED + 2 * KR)
            act.activation(XG[:, KR:2 * KR, :], XG[:, KR:2 * KR, :], ACT.Gelu_apprx_tanh).then_inc(gelu_done, 1)

            def group(g, first, dest):
                for m in range(2):
                    for jj in range(4 * m, 4 * m + 4):
                        act.wait_ge(groups_done, g * 8 + (G_QK + first * 8 + jj + 1))
                        act.activation(dest(g, jj), bank[jj % 4][:, 0:T], ACT.Copy).then_inc(act_evac, 1)
                    if m == 0:
                        act.wait_ge(group_done, g + (first + 1))
                    for j in range(GT):
                        act.wait_ge(gate_mm, g * (2 * GT) + (GATE_SEED + first * 2 * GT + m * GT + j + 1))
                        b0 = (V_AB, V_XB)[m] + first * GT + j
                        act.activation(RT[j] if m == 0 else AB[:, j, :], bank[4 + j % 4][:, 0:CONV], ACT.Sigmoid,
                                       bias=vec[:, bass.ds(g * GT + b0, 1)]).then_inc(gate_evac, 1)
                act.wait_ge(gated, g + (first + 1))
                act.wait_ge(gate_evac, g * (2 * GT) + (SEED + (first + 1) * 2 * GT))
                for j in range(GT):
                    c_ = CL[:, bass.ds(g * GT + (first * GT + j), 1)]
                    own.step(act.activation(AB[:, j, :], RT[j], ACT.Exp, scale=c_), beside=gelu_done)
                for j in range(GT):
                    c_ = CL[:, bass.ds(g * GT + (first * GT + j), 1)]
                    last = act.activation(RT[j], RT[j], ACT.Tanh, scale=c_)
                last.then_inc(a_ready, 1)
                act.wait_ge(sq_ready, g + (first + 1))
                for j in range(GT):
                    last = act.activation(RT[j], RT[j], ACT.Sqrt, scale=-1.0)
                last.then_inc(sqrt_done, 1)

            with act.Fori(0, 2) as g:
                own.enter(g, GT)
                group(g, 0, lambda g, jj: HB[:, jj, bass.ds(g * T, T)])
            own.leave(2)
            with act.Fori(0, 2) as g:
                own.enter(g, GT)
                group(g, 2, lambda g, jj: OG[:, bass.ds(g * 8 + jj, 1), :].rearrange("p a t -> p (a t)"))
            own.leave(2)

            act.wait_ge(z_abs, 1)
            act.activation(t0, t0, ACT.Exp, scale=-1.0).then_inc(z_exp, 1)
            act.wait_ge(mrow_ready, 1)
            act.activation(expnm[0:NH], t1, ACT.Exp, scale=-1.0)
            act.activation(wp[:, 0:TP], gg[:, 0:TP], ACT.Exp, bias=negM[0:NH, TP - 1:TP])
            act.activation(ws[:, TP:T], gg[:, TP:T], ACT.Exp, bias=negM[0:NH, T - 1:T])
            act.activation(gates8[:, 1:2], gates8[:, 0:1], ACT.Exp, bias=negM[0:NH, T - 1:T]).then_inc(row_exp, 1)
            act.wait_ge(act_evac, SEED + 8 * G)
            act.activation(OGf[:, :], OGf[:, :], ACT.Sigmoid).then_inc(og_ready, 1)

            act.wait_ge(gt_ready, 1)
            with act.Fori(0, NH // 2) as hp:
                for e in range(2):
                    h = hp * 2 + e
                    h1 = hp * 2 + (e + 1)

                    def merge_tile(j):
                        wait_apart(act, gt_ready, groups_done, hp * 8 + (G_MG + 4 * e + j + 1))
                        act.activation(HB[:, bass.ds(h, 1), j * T:(j + 1) * T].rearrange("p a t -> p (a t)"),
                                       bank[j][:, 0:T], ACT.Copy).then_inc(act_evac, 1)
                    act.wait_ge(pe_kt, h1)
                    act.activation(kh, HB[:, bass.ds(h, 1), T:2 * T].rearrange("p a t -> p (a t)"), ACT.Copy,
                                   scale=float(DQK) ** -0.5).then_inc(staged_a, 1)
                    act.wait_ge(staged_d, h1)
                    act.wait_ge(staged_a, h1)
                    merge_tile(0)
                    act.wait_ge(pe_scores, hp * 2 + (e + 2))
                    act.activation(es, bank[6][:, 0:T], ACT.Copy).then_inc(es_ready, 1)
                    act.wait_ge(d_ready, h1)
                    act.activation(small2[:, :], bank[5][:, TP:T], ACT.Exp,
                                   bias=hb16[:, bass.ds(h + NH, 1)]).then_inc(wi_ready, 1)
                    for i, (rows_, c, n, t) in enumerate(SC):
                        last = act.activation(dw[0:rows_, c:c + n], dw[0:rows_, c:c + n], ACT.Exp,
                                              bias=gtok[0:rows_, i, bass.ds(h, 1)])
                    last.then_inc(w_ready, 1)
                    merge_tile(1)
                    act.wait_ge(h_ready, h1)
                    act.activation(sq, hh, ACT.Square).then_inc(sq_h, 1)
                    merge_tile(2)
                    act.wait_ge(vr_ready, h1)
                    act.activation(rd, rd, ACT.Sqrt).then_inc(sr_ready, 1)
                    merge_tile(3)
            act.wait_ge(act_evac, SEED + 8 * G + 2 * KD)
            T_PM = TURNS - 2 * (KD // 8)
            T_PR = T_PM - KD // 4
            act.wait_ge(head_done, NH)
            act.wait_ge(pe_cn, NH + 1)
            act.wait_ge(group_done, G + 1)
            act.wait_ge(groups_done, G_PR)
            for n in range(KD):
                act.wait_ge(slot_full[n % 4], (T_PR + n // 4 + 1) * 16)
                for c in range(4):
                    if n == 0:
                        for k in range(c * KQ, (c + 1) * KQ):
                            if k == FREE_EARLY:
                                act.wait_ge(cn_stored, 32 * NH)
                            act.activation(yr_high[:, k, :], XG[:, KR + k, 0:T], ACT.Copy).then_inc(yr_split, 1)
                    elif c < 3:
                        act.wait_ge(q_used, 3 * (n - 1) + c + 1)
                    else:
                        act.wait_ge(groups_done, G_PR + n)
                    act.activation(q_high[c], quarter(w_raw[n % 4], c), ACT.Copy).then_inc(q_split, 1)
                if n < NH:
                    act.activation(HB[:, n, 0:4 * T], HB[:, n, 0:4 * T], ACT.Sigmoid).then_inc(mg_ready, 1)
                act.activation(x_high[:, n, :], OG[:, n, :], ACT.Copy).then_inc(ym_split, 1)
            act.wait_ge(groups_done, G_PM)

            def split_late(n, turn):
                jj = n % 8
                if jj % 2 == 0:
                    act.wait_ge(slot_full[jj // 2], (turn + n // 8 + 1) * 16)
                act.wait_ge(groups_done, G_PM + n - 1)
                act.activation(p_high[jj % 2], tile_of(w_raw[jj // 2], jj % 2), ACT.Copy).then_inc(t_split, 1)

            def split_mixed(n):
                act.wait_ge(dve_evac, SEED + 2 * KR + 24 + KD + n + 1)
                c = slice((n % 4) * T, (n % 4 + 1) * T)
                act.activation(hb_rounded[:, NH // 2 + n // 4, c], HB[:, n // 4, c], ACT.Copy).then_inc(mix_split, 1)

            for n in range(KD):
                split_late(n, T_PM)
                if n == 1:
                    load_x(xr_loaded)
                if n >= 2:
                    split_mixed(n - 2)
            split_mixed(KD - 2)
            split_mixed(KD - 1)
            for n in range(KD, KD + 3):
                split_late(n, T_PM)
            act.wait_ge(groups_done, G_OUT)
            act.dma_start(nb2, bcast(A["norm2_w"][0])).then_inc(nb_loaded, 16)
            act.dma_start(nbf, bcast(A["norm_f_w"])).then_inc(nb_loaded, 16)
            act.dma_start(brt[:, 0:NG], bcast(A["b_router_group"][0])).then_inc(nb_loaded, 16)
            act.dma_start(brt[:, NG:NG + NE], bcast(A["b_router_expert"][0])).then_inc(nb_loaded, 16)
            for n in range(KD + 3, 2 * KD):
                split_late(n, T_PM)
            act.wait_ge(groups_done, G_MOE)
            for i, (t, n) in enumerate(TT):
                act.wait_ge(x2_ready, (i + 1) * (KD // 4))
                act.activation(junk2[0:n], xtok[0:n, i, :], ACT.Square, accum_out=small[0:n, 9 + i:10 + i]).then_inc(ss2_done, 1)
                act.wait_ge(ss2_done, i + 1)
            act.wait_ge(var2, 1)
            act.activation(small[:, 12:15], small[:, 12:15], ACT.Sqrt).then_inc(std2, 1)
            act.wait_ge(cols_e, 1)
            act.activation(gkey, gkey, ACT.Exp)
            act.activation(ex, ex, ACT.Exp).then_inc(exps_e, 1)

            act.sem_inc(gu_copied, 2)
            act.wait_ge(rounds_ready, 1)
            act.wait_ge(xn2_stored, 16 * 3)
            nr = act.value_load(nrounds[0:1, 0:1], min_val=1, max_val=MAXR)

            def split_weights(p, ru):
                b = ru % 4
                act.wait_ge(slot_full[b], (p * 3 + (ru // 4 + LOADS_MOE[b] + 1)) * 16)
                for c in range(2):
                    if c == 0:
                        act.wait_ge(halves_used, p * 12 + (ru + 1))
                    else:
                        act.wait_ge(groups_done, p * 12 + (G_MOE + ru - 1))
                    act.activation(w_high[(2 * ru + c) % 4], half(w_raw[b], ru, c), ACT.Copy).then_inc(w_split, 1)

            def split_rows(p1):
                act.wait_ge(rows_t_done, p1)
                for b in range(4):
                    act.activation(xs[:, 4 * b:4 * b + 4, :, 0:CAP],
                                   bank[b][:, :].rearrange("p (k e c) -> p k e c", k=4, e=2), ACT.Copy).then_inc(xs_high, 1)

            def copy_gu(p, e, c):
                act.wait_ge(groups_done, p * 12 + (G_MOE + 6 * e + 2 * c + 2))
                if c == 0:
                    act.wait_ge(gu_summed, p * 2 + (e + 1))
                act.activation(gu[:, c, :], bank[4 + c][:, 0:DE], ACT.Copy).then_inc(gu_copied, 1)

            act.sem_inc(gu_summed, 1)
            split_weights(0, 0)
            split_rows(1)
            with act.Fori(0, nr * NPAIR) as p:
                for e in range(2):
                    for u in range(1, 4):
                        split_weights(p, 6 * e + u)
                    copy_gu(p, e, 0)
                    split_weights(p, 6 * e + 4)
                    copy_gu(p, e, 1)
                    act.wait_ge(gu_summed, p * 2 + (e + 2))
                    act.wait_ge(h_act, p * 2 + (e + 1))
                    act.activation(sg, bank[6][:, 0:HC], ACT.Silu).then_inc(silu_done, 1)
                    if e == 1:
                        split_rows(p + 2)
                    split_weights(p, 6 * e + 5)
                    split_weights(p, 6 * e + 6)

            for i, (t, n) in enumerate(TT):
                act.wait_ge(fin_ss, i + 1)
                act.activation(y1[0:n, i, :], xtok[0:n, i, :], ACT.Square, accum_out=small[0:n, 18 + i:19 + i]).then_inc(fin_sq, 1)
            act.wait_ge(fin_var, 1)
            act.activation(small[:, 21:24], small[:, 21:24], ACT.Sqrt).then_inc(fin_std, 1)

        @block.vector
        def _(v):
            own = Steps(v, dve_steps)
            step = own.step

            def log1p(e, s, s2, p):
                step(v.tensor_scalar(s, e, 2.0, None, ALU.add))
                step(v.reciprocal(s, s))
                step(v.tensor_tensor(s, s, e, ALU.mult))
                step(v.tensor_tensor(s2, s, s, ALU.mult))
                step(v.tensor_scalar(p, s2, 1.0 / 15, None, ALU.mult))
                for c in (13, 11, 9, 7, 5, 3):
                    step(v.scalar_tensor_tensor(out=p, in0=p, scalar=1.0 / c, in1=s2, op0=ALU.add, op1=ALU.mult))
                step(v.scalar_tensor_tensor(out=p, in0=p, scalar=1.0, in1=s, op0=ALU.add, op1=ALU.mult))
                step(v.tensor_scalar(p, p, 2.0, None, ALU.mult))

            def root_mean(a, b, n_, ready, rooted):
                v.tensor_scalar(small[:, b:b + 3], small[:, a:a + 3], 1.0 / n_, EPS, ALU.mult, ALU.add).then_inc(ready, 1)
                v.wait_ge(rooted, 1)

            v.sem_inc(cn_ready, 1)
            v.memset(small[:, :], 1.0).then_inc(ss_init, 1)
            v.wait_ge(vec_transposed, 1)
            for c, n in ((0, P), (1, VB_ROWS), (2, VC_ROWS)):
                last = v.tensor_copy(vec[:, c * P:c * P + n], bank[4][:, c * P:c * P + n])
            last.then_inc(vec_ready, 1)
            v.wait_ge(ss_done, 3)
            root_mean(0, 3, DM, var_ready, std_ready)
            step(v.reciprocal(small[:, 6:9], small[:, 3:6]))
            for i, (t, n) in enumerate(TT):
                v.tensor_scalar(xntok[0:n, i, :], xtok[0:n, i, :], small[0:n, 6 + i:7 + i], None, ALU.mult).then_inc(xn_ready, 1)
            v.wait_ge(vec_ready, 1)
            lam = vec[:, V_LM:V_LM + KR]
            v.scalar_tensor_tensor(out=AB[:, 0, 0:KR], in0=lam, scalar=-1.0, in1=lam, op0=ALU.mult, op1=ALU.max).then_inc(lam_abs, 1)

            def rest_of_tile(i, jj):
                v.wait_ge(t_split, i * 8 + (jj + 1))
                v.tensor_tensor(tile_of(w_low[jj // 2], jj % 2), tile_of(w_raw[jj // 2], jj % 2),
                                t_high[jj % 2].bitcast(F32), ALU.subtract).then_inc(t_rest, 1)

            rest_of_tile(0, 0)

            def rest_of_x(k):
                v.wait_ge(xn_split, k + 1)
                v.tensor_tensor(x_low[:, k, :], OG[:, k, :], x_high[:, k, :].bitcast(F32), ALU.subtract).then_inc(xnt_ready, 1)

            for k in range(KD):
                v.wait_ge(x_transposed, k + 1)
                v.tensor_scalar(OG[:, k, :], bank[k % 4][:, 0:T], vec[:, V_N1 + k:V_N1 + k + 1], None, ALU.mult).then_inc(xn_made, 1)
                if k > 0:
                    rest_of_x(k - 1)
            rest_of_x(KD - 1)
            v.sem_inc(dve_evac, SEED)
            v.memset(XG[:, :, 0:CW - 1], 0.0)
            step(v.memset(XG[:, :, S0:S0 + CW - 1], 0.0))
            step(v.tensor_copy(XG[:, 0:KR, S0:S0 + CW - 1],
                               vec[:, V_CS:V_CS + VC_ROWS].rearrange("p (w k) -> p k w", k=KR)))

            def xg_out(done, jj):
                v.wait_ge(groups_done, done)
                dst = XG[:, bass.ds(done - 1, 1), :].rearrange("p a t -> p (a t)")
                v.tensor_copy(dst[:, CW - 1:CW - 1 + TP], bank[jj % 4][:, 0:TP])
                v.tensor_copy(dst[:, S0 + CW - 1:PADDED], bank[jj % 4][:, TP:T]).then_inc(dve_evac, 1)

            for jj in range(8):
                if jj > 0:
                    rest_of_tile(0, jj)
                    xg_out(jj, jj - 1)
            with v.Fori(0, 2 * KR // 8 - 1) as i:
                for jj in range(8):
                    rest_of_tile(i + 1, jj)
                    xg_out(i * 8 + (8 + jj), (jj - 1) % 4)
            xg_out(2 * KR, (2 * KR - 1) % 4)
            v.tensor_tensor(XNT[:, :, :], x_high.bitcast(F32), x_low.bitcast(F32), ALU.add).then_inc(xnt_whole, 1)

            v.wait_ge(lam_exp, 1)
            log1p(AB[:, 0, 0:KR], AB[:, 0, KR:2 * KR], AB[:, 0, 2 * KR:3 * KR], CL[:, :])
            step(v.tensor_scalar(AB[:, 0, 0:KR], lam, -1.0, 0.0, ALU.mult, ALU.max))
            step(v.tensor_tensor(CL[:, :], CL[:, :], AB[:, 0, 0:KR], ALU.add))
            step(v.tensor_scalar(CL[:, :], CL[:, :], -8.0, None, ALU.mult))
            v.sem_inc(group_done, 1)
            v.wait_ge(dve_evac, SEED + 2 * KR)
            for c, first in ((0, TP), (1, PADDED - (CW - 1))):
                last = v.tensor_copy(ST[:, c, KR:].rearrange("p (w k) -> p k w", k=KR), XG[:, 0:KR, first:first + CW - 1])
            last.then_inc(states_saved, 1)
            v.wait_ge(states_saved, 1)
            with v.Fori(0, KR) as k:
                own.enter(k, CW - 1)
                xr = XG[:, bass.ds(k, 1), :].rearrange("p a t -> p (a t)")

                def tap(w):
                    return vec[:, bass.ds(k + (V_CW + w * KR), 1)]
                step(v.tensor_scalar(tmp, xr[:, 0:CONV], tap(0), vec[:, bass.ds(k + V_CB, 1)], ALU.mult, ALU.add))
                for w in range(1, CW - 1):
                    step(v.scalar_tensor_tensor(out=tmp, in0=xr[:, w:w + CONV], scalar=tap(w), in1=tmp, op0=ALU.mult, op1=ALU.add))
                v.scalar_tensor_tensor(out=xr[:, 0:CONV], in0=xr[:, CW - 1:CW - 1 + CONV], scalar=tap(CW - 1), in1=tmp,
                                       op0=ALU.mult, op1=ALU.add).then_inc(conv_done, 1)
                v.wait_ge(conv_done, k + 1)
            own.leave(KR)
            v.wait_ge(conv_done, KR)

            v.wait_ge(gelu_done, 1)
            with v.Fori(0, G) as g:
                own.enter(g, 6 * GT + 1)
                XC = XG[:, bass.ds(g * GT, GT), :]
                YR = XG[:, bass.ds(g * GT + KR, GT), :]
                v.wait_ge(gate_evac, g * (2 * GT) + (SEED + 2 * GT))
                v.tensor_tensor(XC[:, :, 0:CONV], XC[:, :, 0:CONV], AB[:, :, :], ALU.mult).then_inc(gated, 1)
                v.wait_ge(a_ready, g + 1)
                for j in range(GT):
                    step(v.tensor_tensor(tmp, AB[:, j, :], AB[:, j, :], ALU.mult))
                    last = v.scalar_tensor_tensor(out=RT[j], in0=tmp, scalar=1.0, in1=RT[j], op0=ALU.add, op1=ALU.mult)
                    if j < GT - 1:
                        step(last)
                last.then_inc(sq_ready, 1)
                v.wait_ge(sqrt_done, g + 1)
                for j in range(GT):
                    step(v.tensor_tensor(XC[:, j, 0:CONV], XC[:, j, 0:CONV], RT[j], ALU.mult))
                step(v.memset(AB[:, :, S0 - 1:S0], 0.0))
                step(v.tensor_copy(XC[:, :, S0 - 1:S0], vec[:, bass.ds(g * GT + V_H0, GT)].rearrange("p (k a) -> p k a", a=1)))
                for j in range(GT):
                    step(v.tensor_tensor_scan(RT[j], AB[:, j, :], XC[:, j, 0:CONV], 0.0, ALU.mult, ALU.add))
                for j in range(GT):
                    for c, col in ((0, TP - 1), (1, CONV - 1)):
                        v.tensor_copy(ST[:, c, bass.ds(g * GT + j, 1)], RT[j][:, col:col + 1])
                    step(v.tensor_tensor(YR[:, j, 0:TP], YR[:, j, CW - 1:CW - 1 + TP], RT[j][:, 0:TP], ALU.mult))
                for j in range(GT):
                    step(v.tensor_tensor(YR[:, j, TP:T], YR[:, j, S0 + CW - 1:PADDED], RT[j][:, S0:CONV], ALU.mult))
                v.sem_inc(group_done, 1)
            own.leave(G)

            v.wait_ge(gif_done, 2)
            v.tensor_scalar(li, bank[4][0:NH, 0:T], gates8[:, 2:3], None, ALU.add)
            step(v.tensor_scalar(lf, bank[5][0:NH, 0:T], gates8[:, 3:4], None, ALU.add))
            v.scalar_tensor_tensor(out=t0, in0=lf, scalar=-1.0, in1=lf, op0=ALU.mult, op1=ALU.max).then_inc(z_abs, 1)
            v.wait_ge(z_exp, 1)
            log1p(t0, bc, gg, wp)
            step(v.scalar_tensor_tensor(out=lf, in0=lf, scalar=0.0, in1=wp, op0=ALU.min, op1=ALU.subtract))
            step(v.memset(t1, 1.0))
            v.tensor_tensor_scan(bc[:, 0:TP], t1[:, 0:TP], lf[:, 0:TP], 0.0, ALU.mult, ALU.add)
            step(v.tensor_tensor_scan(bc[:, TP:T], t1[:, TP:T], lf[:, TP:T], 0.0, ALU.mult, ALU.add))
            step(v.tensor_tensor(gg, li, bc, ALU.subtract))
            v.tensor_tensor_scan(t0[:, 0:TP], gg[:, 0:TP], gg[:, 0:TP], 0.0, ALU.max, ALU.max)
            step(v.tensor_tensor_scan(t0[:, TP:T], gg[:, TP:T], gg[:, TP:T], gates8[:, 0:1], ALU.max, ALU.max))
            v.tensor_scalar(negM[0:NH], t0, -1.0, None, ALU.mult)
            step(v.tensor_tensor(t1, bc, t0, ALU.add))
            v.tensor_copy(gates8[:, 4:5], t1[:, TP - 1:TP])
            v.tensor_copy(gates8[:, 5:6], t1[:, T - 1:T])
            v.memset(wp, 0.0)
            v.memset(ws, 0.0).then_inc(mrow_ready, 1)
            v.wait_ge(row_exp, 1)
            v.tensor_scalar(diag8[:, 0:NH], ident[0:NH, 0:NH], gates8[:, 1:2], None, ALU.mult)
            v.tensor_scalar(diag8[:, NH:2 * NH], ident[0:NH, 0:NH], gates8[:, 0:1], None, ALU.mult).then_inc(rows_t, 1)

            with v.Fori(0, 2) as i:
                for b in range(4):
                    for c, (t, n) in enumerate(TT):
                        jj = 3 * b + c
                        v.wait_ge(groups_done, i * 12 + (G_V + jj + 1))
                        dst = HB[0:n, bass.ds(i * 4 + b, 1), HV0 + c * DV:HV0 + (c + 1) * DV].rearrange("p a t -> p (a t)")
                        v.tensor_copy(dst, bank[jj % 4][0:n, 0:DV]).then_inc(dve_evac, 1)
            v.wait_ge(gt_mm, 1)
            for i, (t, n) in enumerate(TT):
                v.tensor_copy(gtok[0:n, i, :], bank[6][0:n, i * 3 * NH:(i + 1) * 3 * NH])
            v.tensor_copy(hb16[:, :], bank[7][:, 0:2 * NH]).then_inc(gt_ready, 1)
            v.wait_ge(gt_ready, 1)
            v.wait_ge(og_ready, 1)
            v.wait_ge(dve_evac, SEED + 2 * KR + 24)

            with v.Fori(0, NH) as h:
                own.enter(h, 8)
                h1 = h + 1

                def col(a, c0_, n=P):
                    return a[0:n, bass.ds(h + c0_, 1)]
                v.wait_ge(pe_scores, h1)
                v.wait_ge(pe_ss, h1)
                v.wait_ge(pe_cn, h1)
                v.tensor_scalar(selM[0:NH], negM[0:NH], ident[0:NH, bass.ds(h, 1)], None, ALU.mult)
                v.tensor_scalar(selE[0:NH], expnm[0:NH], ident[0:NH, bass.ds(h, 1)], None, ALU.mult)
                v.tensor_scalar(n0b, ones[:, :], col(nst, 2 * NH), None, ALU.mult)
                hb = HB[:, bass.ds(h, 1), :].rearrange("p a t -> p (a t)")
                v.tensor_copy(vh[:, 0:2 * DV], hb[:, HV0:HV0 + 2 * DV])
                v.tensor_copy(vh[0:NL, 2 * DV:3 * DV], hb[0:NL, HV0 + 2 * DV:HV0 + 3 * DV])
                v.tensor_copy(qh, hb[:, 0:T]).then_inc(staged_d, 1)
                v.wait_ge(pe_scores, h + 2)
                v.tensor_tensor(dw[:, 0:TP], bank[5][:, 0:TP], tri[:, 0:TP], ALU.add)
                v.tensor_tensor(dw[:, TP:2 * TP - P], bank[5][:, P:TP], tri[:, 0:TP - P], ALU.add)
                c = SC[2][1]
                v.tensor_tensor(dw[0:NL, c:c + NL], bank[5][0:NL, 2 * P:T], trl[:, :], ALU.add).then_inc(d_ready, 1)
                v.wait_ge(staged_d, h1)
                v.wait_ge(wi_ready, h1)
                step(v.tensor_tensor(small2[:, :], small2[:, :], qh[:, TP:T], ALU.mult))
                v.wait_ge(w_ready, h1)
                v.tensor_tensor(dw[:, 0:c], dw[:, 0:c], bank[4][:, 0:c], ALU.mult)
                v.tensor_tensor(dw[0:NL, c:c + NL], dw[0:NL, c:c + NL], bank[4][0:NL, c:c + NL], ALU.mult).then_inc(sw_ready, 1)
                v.wait_ge(pe_num, h + 2)
                v.wait_ge(es_ready, h1)
                step(v.scalar_tensor_tensor(out=rd, in0=bank[5][:, 0:T], scalar=-1.0, in1=es, op0=ALU.mult, op1=ALU.max))
                step(v.tensor_tensor(rd, rd, bank[5][:, 0:T], ALU.max))
                step(v.reciprocal(rd, rd))
                v.tensor_tensor(hh[:, 0:T], bank[6][:, 0:T], rd, ALU.mult)
                v.tensor_tensor(hh[:, T:2 * T], bank[7][:, 0:T], rd, ALU.mult).then_inc(h_ready, 1)
                v.wait_ge(pe_kt, h + 2)
                for i, (t, n) in enumerate(TT):
                    v.tensor_scalar(kp[0:n, i * DQK:(i + 1) * DQK], bank[4][0:n, i * P:i * P + DQK],
                                    gtok[0:n, i, bass.ds(h + NH, 1)], None, ALU.mult)
                v.tensor_scalar(ks[0:NL], bank[4][0:NL, 2 * P:2 * P + DQK],
                                gtok[0:NL, 2, bass.ds(h + 2 * NH, 1)], None, ALU.mult).then_inc(kp_ready, 1)
                v.wait_ge(pe_ss, h + 2)
                v.wait_ge(h_ready, h1)
                v.tensor_scalar(rd, bank[5][:, 0:T], 1.0 / DV, EPS, ALU.mult, ALU.add).then_inc(vr_ready, 1)
                v.wait_ge(sr_ready, h1)
                step(v.reciprocal(rd, rd))
                for c in range(2):
                    last = v.scalar_tensor_tensor(out=hh[:, c * T:(c + 1) * T], in0=hh[:, c * T:(c + 1) * T],
                                                  scalar=vec[:, bass.ds(h * 2 + (V_MN + c), 1)], in1=rd, op0=ALU.mult, op1=ALU.mult)
                step(last)
                og = OG[:, bass.ds(h * 2, 2), :].rearrange("p a t -> p (a t)")
                v.tensor_tensor(og, og, hh, ALU.mult).then_inc(head_done, 1)
                v.wait_ge(pe_cn, h + 2)
                v.tensor_copy(cn[:, 0:DV], bank[6][:, 0:DV])
                step(v.tensor_copy(nst[:, bass.ds(h, 1)], bank[7][:, 0:1]))
                step(v.scalar_tensor_tensor(out=nst[:, bass.ds(h + NH, 1)], in0=col(nst, 2 * NH), scalar=col(hb16, 0),
                                            in1=bank[7][:, 1:2], op0=ALU.mult, op1=ALU.add))
                v.scalar_tensor_tensor(out=cn[:, DV:2 * DV], in0=c0, scalar=col(hb16, 0), in1=bank[6][:, DV:2 * DV],
                                       op0=ALU.mult, op1=ALU.add).then_inc(cn_ready, 1)
            own.leave(NH)

            def gate_r(n):
                v.wait_ge(mg_ready, n // 4 + 1)
                v.wait_ge(groups_done, G_PR + n + 1)
                m = HB[:, n // 4, (n % 4) * T:(n % 4 + 1) * T]
                v.tensor_tensor(m, m, bank[n % 4][:, 0:T], ALU.mult).then_inc(dve_evac, 1)

            for n in range(KD):
                for c in range(4):
                    if n == 0:
                        for k in range(c * KQ, (c + 1) * KQ):
                            v.wait_ge(yr_split, k + 1)
                            v.tensor_tensor(xg_rounded[:, KR + k, 0:T], XG[:, KR + k, 0:T], yr_high[:, k, :].bitcast(F32),
                                            ALU.subtract).then_inc(yr_rest, 1)
                    v.wait_ge(q_split, 4 * n + c + 1)
                    v.tensor_tensor(quarter(w_low[n % 4], c), quarter(w_raw[n % 4], c), q_high[c].bitcast(F32),
                                    ALU.subtract).then_inc(q_rest, 1)
                v.wait_ge(ym_split, n + 1)
                v.tensor_tensor(x_low[:, n, :], OG[:, n, :], x_high[:, n, :].bitcast(F32), ALU.subtract).then_inc(ym_rest, 1)
                if n >= 1:
                    gate_r(n - 1)
            gate_r(KD - 1)

            v.wait_ge(dve_evac, SEED + 2 * KR + 24 + KD)

            def rest_of_late(n):
                jj = n % 8
                v.wait_ge(t_split, 2 * KR + n + 1)
                v.tensor_tensor(tile_of(w_low[jj // 2], jj % 2), tile_of(w_raw[jj // 2], jj % 2),
                                p_high[jj % 2].bitcast(F32), ALU.subtract).then_inc(t_rest, 1)

            def merge(n):
                v.wait_ge(mg_ready, KD // 4 + n // 4 + 1)
                v.wait_ge(groups_done, G_PM + n + 1)
                c = slice((n % 4) * T, (n % 4 + 1) * T)
                m, r_ = HB[:, NH // 2 + n // 4, c], HB[:, n // 4, c]
                step(v.tensor_tensor(m, m, bank[n % 4][:, 0:T], ALU.mult))
                v.tensor_tensor(r_, r_, m, ALU.add).then_inc(dve_evac, 1)

            def rest_of_mixed(n):
                v.wait_ge(mix_split, n + 1)
                c = slice((n % 4) * T, (n % 4 + 1) * T)
                v.tensor_tensor(hb_rounded[:, n // 4, c], HB[:, n // 4, c], hb_rounded[:, NH // 2 + n // 4, c].bitcast(F32),
                                ALU.subtract).then_inc(mix_rest, 1)

            for n in range(KD):
                rest_of_late(n)
                if n >= 1:
                    merge(n - 1)
                if n >= 2:
                    rest_of_mixed(n - 2)
            merge(KD - 1)
            rest_of_mixed(KD - 2)
            rest_of_mixed(KD - 1)

            def block_out(n):
                v.wait_ge(groups_done, G_OUT + n + 1)
                v.tensor_copy(XNT[:, n, :], bank[n % 4][:, 0:T]).then_inc(dve_evac, 1)

            for n in range(KD):
                rest_of_late(KD + n)
                if n >= 1:
                    block_out(n - 1)
            block_out(KD - 1)
            v.wait_ge(st_t, 1)
            for c in range(2):
                last = v.tensor_copy(vec[0:CW * KR, c * P:(c + 1) * P], bank[4 + c][0:CW * KR, 0:P])
            last.then_inc(st_ready, 1)
            v.wait_ge(xr_loaded, 16 * 5)
            for i, (t, n) in enumerate(TT):
                for q in range(KD // 4):
                    u = i * (KD // 4) + q
                    v.wait_ge(x2_t, u + 1)
                    c = slice(q * 4 * P, (q + 1) * 4 * P)
                    v.tensor_tensor(xtok[0:n, i, c], xtok[0:n, i, c], bank[u % 4][0:n, :], ALU.add).then_inc(x2_ready, 1)
            v.wait_ge(ss2_done, 3)
            root_mean(9, 12, DM, var2, std2)
            step(v.reciprocal(small[:, 15:18], small[:, 12:15]))
            v.wait_ge(nb_loaded, 16 * 4)
            for i, (t, n) in enumerate(TT):
                v.scalar_tensor_tensor(out=xntok[0:n, i, :], in0=xtok[0:n, i, :], scalar=small[0:n, 15 + i:16 + i],
                                       in1=nb2[0:n], op0=ALU.mult, op1=ALU.mult).then_inc(xn2_ready, 1)
            for k in range(KD):
                v.wait_ge(xn2_t, k + 1)
                v.tensor_copy(xn2t[:, k, :], bank[k % 4][:, 0:T]).then_inc(xn2t_ready, 1)

            v.memset(gl, 0.0)
            v.memset(el, 0.0)
            step(v.memset(rk, 0.0))
            v.wait_ge(logits, 1)
            R = NG + NE
            for i, (t, n) in enumerate(TT):
                v.tensor_tensor(gl[0:n, i, :], bank[4][0:n, i * R:i * R + NG], brt[0:n, 0:NG], ALU.add)
                last = v.tensor_tensor(el[0:n, i, :], bank[4][0:n, i * R + NG:(i + 1) * R], brt[0:n, NG:R], ALU.add)
            step(last)

            def wide_(a, n):
                return a.broadcast_to([P, 3, n])

            def first_max(x, key, mx, oh):
                step(v.tensor_reduce(mx, x, AX.X, ALU.max))
                step(v.tensor_tensor(key, x, wide_(mx, NG), ALU.is_equal))
                kj = kc[:, NE:NE + EG].rearrange("p (a j) -> p a j", a=1).broadcast_to([P, 3, EG])
                step(v.tensor_tensor(key, key, kj, ALU.mult))
                step(v.tensor_reduce(kmx, key, AX.X, ALU.max))
                step(v.tensor_tensor(oh, key, wide_(kmx, NG), ALU.is_equal))
            first_max(gl, gkey, gmx, goh)
            step(v.tensor_tensor(gkey, gl, wide_(gmx, NG), ALU.subtract))
            pg = prod.rearrange("p a (g j) -> p (a g) j", g=NG)
            step(v.tensor_tensor(pg, el.rearrange("p a (g j) -> p (a g) j", g=NG),
                                 goh.rearrange("p a (g o) -> p (a g) o", o=1).broadcast_to([P, 3 * NG, EG]), ALU.mult))
            step(v.tensor_reduce(ein, prod.rearrange("p a (g j) -> p a j g", g=NG), AX.X, ALU.add))
            first_max(ein, ekey, v1, o1)
            step(v.scalar_tensor_tensor(out=e2, in0=o1, scalar=NEG, in1=ein, op0=ALU.mult, op1=ALU.add))
            first_max(e2, ekey, v2, o2)
            v.tensor_tensor(ex, v2, v1, ALU.subtract).then_inc(cols_e, 1)
            for E_, o_ in ((E1, o1), (E2, o2)):
                for i in range(3):
                    last = v.tensor_tensor(E_[:, i, :].rearrange("p (g j) -> p g j", g=NG),
                                           goh[:, i, :].rearrange("p (g o) -> p g o", o=1).broadcast_to([P, NG, EG]),
                                           o_[:, i, :].rearrange("p (o j) -> p o j", o=1).broadcast_to([P, NG, EG]), ALU.mult)
            step(last)
            v.tensor_tensor(picked, E1, E2, ALU.add).then_inc(chosen, 1)
            v.wait_ge(exps_e, 1)
            step(v.tensor_reduce(gw, gkey, AX.X, ALU.add))
            step(v.tensor_scalar(w1, ex, 1.0, None, ALU.add))
            step(v.tensor_tensor(w1, w1, gw, ALU.mult))
            step(v.reciprocal(w1, w1))
            step(v.tensor_tensor(w2, ex, w1, ALU.mult))
            v.wait_ge(rank_mm, 1)
            for i, (t, n) in enumerate(TT):
                last = v.tensor_copy(rk[0:n, i, :], bank[5][0:n, i * NE:(i + 1) * NE])
            step(last)
            step(v.tensor_tensor(sl, rk, kc[:, 0:NE].rearrange("p (a j) -> p a j", a=1).broadcast_to([P, 3, NE]), ALU.add))
            for m in range(1, MAXR):
                step(v.tensor_scalar(slt, rk, float(m * CAP), float(ROUND_ROWS - CAP), ALU.is_ge, ALU.mult))
                step(v.tensor_tensor(sl, sl, slt, ALU.add))
            for c, E_ in enumerate((E1, E2)):
                step(v.tensor_tensor(slt, E_, sl, ALU.mult))
                step(v.tensor_reduce(slf[:, :, c:c + 1], slt, AX.X, ALU.add))
            step(v.tensor_copy(slot_i[:, :, :], slf.rearrange("p a c -> p c a")))
            step(v.tensor_reduce(cmx[:, 0:1], bank[6][:, 0:NE], AX.X, ALU.max))
            step(v.memset(cmx[:, 1:2], 1.0))
            for m in range(1, MAXR):
                step(v.scalar_tensor_tensor(out=cmx[:, 1:2], in0=cmx[:, 0:1], scalar=float(m * CAP), in1=cmx[:, 1:2],
                                            op0=ALU.is_gt, op1=ALU.add))
            v.tensor_copy(nrounds[:, :], cmx[:, 1:2]).then_inc(rounds_ready, 1)

            v.sem_inc(h_act, 1)
            v.sem_inc(y_out, 1)
            v.wait_ge(rounds_ready, 1)
            nr = v.value_load(nrounds[0:1, 0:1], min_val=1, max_val=MAXR)

            def rest_of_weights(p, ru):
                for c in range(2):
                    v.wait_ge(w_split, p * 24 + (2 * ru + c + 1))
                    v.tensor_tensor(half(w_low[ru % 4], ru, c), half(w_raw[ru % 4], ru, c),
                                    w_high[(2 * ru + c) % 4].bitcast(F32), ALU.subtract).then_inc(w_rest, 1)

            def rest_of_rows(p):
                for b in range(4):
                    v.wait_ge(xs_high, p * 4 + (b + 1))
                    last = v.tensor_tensor(xs[:, 4 * b:4 * b + 4, :, CAP:2 * CAP],
                                           bank[b][:, :].rearrange("p (k e c) -> p k e c", k=4, e=2),
                                           xs[:, 4 * b:4 * b + 4, :, 0:CAP].bitcast(F32), ALU.subtract)
                last.then_inc(xgt_ready, 1)

            rest_of_weights(0, 0)
            for b in range(4):
                v.wait_ge(xs_high, b + 1)
                last = v.tensor_tensor(xs[:, 4 * b:4 * b + 4, :, CAP:2 * CAP],
                                       bank[b][:, :].rearrange("p (k e c) -> p k e c", k=4, e=2),
                                       xs[:, 4 * b:4 * b + 4, :, 0:CAP].bitcast(F32), ALU.subtract)
            last.then_inc(xgt_ready, 1)
            with v.Fori(0, nr * NPAIR) as p:
                for e in range(2):
                    for u in range(1, 5):
                        rest_of_weights(p, 6 * e + u)
                    v.wait_ge(silu_done, p * 2 + (e + 1))
                    v.tensor_tensor(hf, sg, bank[6][:, HC:2 * HC], ALU.mult).then_inc(h_steps, 1)
                    v.wait_ge(h_steps, p * 4 + (2 * e + 1))
                    v.tensor_copy(hs_high, hf).then_inc(h_steps, 1)
                    v.wait_ge(h_steps, p * 4 + (2 * e + 2))
                    v.tensor_tensor(hs_low, hf, hs_high.bitcast(F32), ALU.subtract).then_inc(h_act, 1)
                    if e == 1:
                        rest_of_rows(p + 1)
                    rest_of_weights(p, 6 * e + 5)
                    rest_of_weights(p, 6 * e + 6)
                    v.wait_ge(groups_done, p * 12 + (G_MOE + 6 * e + 6))
                    if e == 0:
                        v.wait_ge(y_free, p + 1)
                    for b in range(4):
                        last = v.tensor_copy(ysb[0:CAP, e, b * DE:(b + 1) * DE], bank[b][0:CAP, 0:DE])
                    last.then_inc(y_out, 1)

            for i, (t, n) in enumerate(TT):
                v.wait_ge(y_loaded[i], 16 * 2)
                step(v.scalar_tensor_tensor(out=xtok[0:n, i, :], in0=y1[0:n, i, :], scalar=w1[0:n, i, :],
                                            in1=xtok[0:n, i, :], op0=ALU.mult, op1=ALU.add))
                v.scalar_tensor_tensor(out=xtok[0:n, i, :], in0=y2[0:n, i, :], scalar=w2[0:n, i, :],
                                       in1=xtok[0:n, i, :], op0=ALU.mult, op1=ALU.add).then_inc(fin_ss, 1)
            v.wait_ge(fin_sq, 3)
            root_mean(18, 21, DM, fin_var, fin_std)
            step(v.reciprocal(small[:, 0:3], small[:, 21:24]))
            for i, (t, n) in enumerate(TT):
                v.scalar_tensor_tensor(out=xtok[0:n, i, :], in0=xtok[0:n, i, :], scalar=small[0:n, i:i + 1],
                                       in1=nbf[0:n], op0=ALU.mult, op1=ALU.mult).then_inc(fin_out, 1)

        @block.gpsimd
        def _(pool):
            own = Steps(pool, pool_steps)
            step = own.step
            pool.memset(ones[:, :], 1.0)
            pool.memset(zeros_i[:, :], 0)
            for e in range(NE):
                pool.memset(kc[:, e:e + 1], float(e * CAP))
            for j in range(EG):
                pool.memset(kc[:, NE + j:NE + j + 1], float(EG - j))
            pool.memset(tri[:, :], 0.0)
            pool.memset(trl[:, :], 0.0)
            step(pool.memset(ident[:, :], 0.0))
            pool.affine_select(out=before[:, :], in_=ones[:, :], compare_op=ALU.is_gt, fill=0.0, base=0,
                               pattern=[[1, P]], channel_multiplier=-1)
            pool.affine_select(out=tri[:, :], in_=tri[:, :], compare_op=ALU.is_ge, fill=NEG, base=0,
                               pattern=[[1, TP]], channel_multiplier=-1)
            step(pool.affine_select(out=trl[:, :], in_=trl[:, :], compare_op=ALU.is_ge, fill=NEG, base=0,
                                    pattern=[[1, NL]], channel_multiplier=-1))
            step(pool.memset(trl[0:PL, PL:NL], NEG))
            pool.iota(tokid[:, :], pattern=[[P, 3]], base=0, channel_multiplier=1)
            pool.affine_select(out=ident[:, :], in_=ident[:, :], compare_op=ALU.not_equal, fill=1.0, base=0,
                               pattern=[[-1, P]], channel_multiplier=1).then_inc(consts_ready, 1)
            pool.wait_ge(consts_ready, 1)
            pool.dma_start(slot_token.rearrange("(p c) o -> p (c o)", p=P), zeros_i[:, :]).then_inc(zeroed, 16)

            pool.wait_ge(vec_ready, 1)
            pool.wait_ge(ss_done, 3)
            for m in range(2):
                for i in range(GT):
                    last = pool.memset(bd[m][i], 0.0)
            step(last)
            with pool.Fori(0, G) as g:
                for m, name in enumerate(("rg_a_w", "rg_x_w")):
                    wait_apart(pool, consts_ready, gate_mm, g * (2 * GT) + (GATE_SEED + m * GT - GT))
                    for b, r, n, i, p0 in PIECES:
                        c = RB * b - (i - 1) * P
                        pool.dma_start(bd[m][i][p0:p0 + n, c:c + RB],
                                       A[name][0, bass.ds(g * BG + b, 1), r:r + n, :].rearrange("a r c -> (a r) c")).then_inc(bd_loaded[m], 16)
            C0 = A["state_mlstm_C"][0, 0]
            pool.wait_ge(gt_ready, 1)
            pool.dma_start(O["p_m"][0].rearrange("a h -> h a"), gates8[:, 4:5], allow_slow_non_contiguous=True).then_inc(out_stored, 16)
            pool.dma_start(O["s_m"][0].rearrange("a h -> h a"), gates8[:, 5:6], allow_slow_non_contiguous=True).then_inc(out_stored, 16)
            with pool.Fori(0, NH) as h:
                pool.wait_ge(cn_ready, h + 1)
                pool.dma_start(c0, C0[bass.ds(h, 1), :, :].rearrange("a k v -> (a k) v")).then_inc(c0_loaded, 16)
                wait_apart(pool, gt_ready, cn_ready, h + 2)
                pool.dma_start(O["p_C"][0, 0][bass.ds(h, 1), :, :].rearrange("a k v -> (a k) v"), cn[:, 0:DV]).then_inc(cn_stored, 16)
                pool.dma_start(O["s_C"][0, 0][bass.ds(h, 1), :, :].rearrange("a k v -> (a k) v"), cn[:, DV:2 * DV]).then_inc(cn_stored, 16)
                pool.wait_ge(cn_stored, h * 32 + 32)
            pool.dma_start(O["p_n"][0, 0].rearrange("h k -> k h"), nst[:, 0:NH], allow_slow_non_contiguous=True).then_inc(out_stored, 16)
            pool.dma_start(O["s_n"][0, 0].rearrange("h k -> k h"), nst[:, NH:2 * NH], allow_slow_non_contiguous=True).then_inc(out_stored, 16)
            pool.wait_ge(st_ready, 1)
            for c, s_ in enumerate("ps"):
                pool.dma_start(O[s_ + "_h"][0].rearrange("a (k f) -> (a k) f", k=KR), vec[0:KR, c * P:(c + 1) * P]).then_inc(out_stored, 16)
                pool.dma_start(O[s_ + "_conv"][0, 0].rearrange("w (k f) -> (w k) f", k=KR),
                               vec[KR:CW * KR, c * P:(c + 1) * P]).then_inc(out_stored, 16)
            pool.wait_ge(xn2_ready, 3)
            for i, (t, n) in enumerate(TT):
                pool.dma_start(xn2_rows[t:t + n, :], xntok[0:n, i, :]).then_inc(xn2_stored, 16)
            pool.wait_ge(zeroed, 16)
            pool.wait_ge(rounds_ready, 1)
            pool.tensor_tensor(add2[:, :], ident[:, 0:CAP], ident[:, CAP:P], ALU.add).then_inc(add2_ready, 1)
            for c in range(2):
                for i, (t, n) in enumerate(TT):
                    pool.indirect_dma_start(out=slot_token[:, :], out_offset=bass.IndirectOffsetOnAxis(ap=slot_i[0:n, c, i:i + 1], axis=0),
                                            in_=tokid[0:n, i:i + 1], in_offset=None).then_inc(perm_written, 16)
            pool.wait_ge(perm_written, 16 * 6)
            pool.wait_ge(xn2_stored, 16 * 3)
            nr = pool.value_load(nrounds[0:1, 0:1], min_val=1, max_val=MAXR)
            with pool.If(nr > 1):
                step(pool.memset(HBf[:, 2 * DM:3 * DM], 0.0))
                with pool.Fori(0, (SLOTS - ROUND_ROWS) // P) as k:
                    pool.dma_start(slot_out[bass.ds(k * P + ROUND_ROWS, P), :], HBf[:, 2 * DM:3 * DM]).then_inc(rest_zeroed, 16)
                pool.wait_ge(rest_zeroed, (SLOTS - ROUND_ROWS) // P * 16)
            with pool.Else():
                pool.nop()

            def gather(p, p1):
                pool.dma_start(gidx[:, :], slot_token[bass.ds(p * P, P), :]).then_inc(idx_loaded, 16)
                wait_apart(pool, rounds_ready, idx_loaded, p1 * 16)
                pool.indirect_dma_start(out=rows, out_offset=None, in_=xn2_rows[:, :],
                                        in_offset=bass.IndirectOffsetOnAxis(ap=gidx[:, :], axis=0)).then_inc(rows_gathered, 16)
            pool.sem_inc(y_free, 1)
            gather(0, 1)
            with pool.Fori(0, nr * NPAIR) as p:
                pool.wait_ge(rows_gathered, (p + 1) * 16)
                pool.wait_ge(rows_t_done, p + 1)
                gather(p + 1, p + 2)
                pool.wait_ge(y_out, p * 2 + 3)
                pool.dma_start(slot_out[bass.ds(p * P, P), :].rearrange("(e s) n -> s e n", e=2), ysb[0:CAP]).then_inc(y_stored, 16)
                pool.wait_ge(y_stored, (p + 1) * 16)
                pool.sem_inc(y_free, 1)
            wait_apart(pool, rounds_ready, y_stored, nr * (NPAIR * 16))
            wait_apart(pool, rounds_ready, rows_gathered, nr * (NPAIR * 16) + 16)
            wait_apart(pool, rounds_ready, xgt_ready, nr * NPAIR + 1)
            wait_apart(pool, rounds_ready, groups_done, nr * (NPAIR * 12) + G_MOE)

            def results(table):
                for i, (t, n) in enumerate(TT):
                    for c, dst in enumerate((y1, y2)):
                        pool.indirect_dma_start(out=dst[0:n, i, :], out_offset=None, in_=table,
                                                in_offset=bass.IndirectOffsetOnAxis(ap=slot_i[0:n, c, i:i + 1], axis=0)).then_inc(y_loaded[i], 16)
            with pool.If(nr > 1):
                results(slot_out[:, :])
            with pool.Else():
                results(slot_out[0:ROUND_ROWS, :])
            pool.wait_ge(fin_out, 3)
            for i, (r, p0, n) in enumerate([(0, NM, P - NM), (P - NM, 0, P), (2 * P - NM, 0, PL)]):
                pool.dma_start(O["y_p"][0, r:r + n, :], xtok[p0:p0 + n, i, :]).then_inc(out_stored, 16)
            pool.dma_start(O["y_s"][0], xtok[PL:NL, 2, :]).then_inc(out_stored, 16)
            pool.wait_ge(cn_stored, 32 * NH)
            pool.wait_ge(out_stored, 16 * 12)


def kernel(**inputs):
    import numpy as np
    import concourse.bacc as bacc
    from concourse import mybir
    from concourse.bass_utils import run_bass_kernel_spmd

    nc = bacc.Bacc("TRN2", target_bir_lowering=False, num_devices=1)
    arrays, A, O = {}, {}, {}
    for name, value in inputs.items():
        a = np.ascontiguousarray(value)
        arrays["in_" + name] = a
        A[name] = nc.dram_tensor("in_" + name, a.shape, mybir.dt.from_np(a.dtype), kind="ExternalInput").ap()
    shapes = {"y_p": inputs["x_prompt"].shape, "y_s": inputs["x_sample"].shape}
    for s, b in (("p", inputs["x_prompt"].shape[0]), ("s", inputs["x_sample"].shape[0])):
        for k, name in (("conv", "state_rglru_conv"), ("h", "state_rglru_h"), ("C", "state_mlstm_C"),
                        ("n", "state_mlstm_n"), ("m", "state_mlstm_m")):
            full = inputs[name].shape
            shapes[s + "_" + k] = (full[0], b) + tuple(full[2:])
    for key, shape in shapes.items():
        O[key] = nc.dram_tensor("out_" + key, tuple(shape), mybir.dt.float32, kind="ExternalOutput").ap()
    build(nc, A, O)
    r = run_bass_kernel_spmd(nc, [arrays], core_ids=[0]).results[0]
    return tuple(r["out_" + key] for key in shapes)
```
